# Optimizing a Trainium2 kernel written in Bass

```python
import math
import jax, jax.numpy as jnp
from jax import lax
import numpy as np

D_MODEL = 2048
BATCH = 1
SEQ = 512
DEPTH = 1
DEC_BATCH = 8
DEC_SEQ = 8
PAST_LEN = 512
PAGE_SIZE = 128

N_ATT_HEADS = 8
ATT_HEAD_DIM = 128
ATT_WIDTH = N_ATT_HEADS * ATT_HEAD_DIM
N_IDX_HEADS = 16
IDX_DIM = 64
TOPK_MAX = 256
N_SSM_HEADS = 16
SSM_HEAD_DIM = 64
SSM_WIDTH = N_SSM_HEADS * SSM_HEAD_DIM
N_SSM_GROUPS = 2
SSM_STATE = 128
CONV_W = 4
CONV_DIM = SSM_WIDTH + 2 * N_SSM_GROUPS * SSM_STATE
SSD_CHUNK = 128
MIX_WIDTH = ATT_WIDTH + SSM_WIDTH
IN_WIDTH = 3 * ATT_WIDTH + N_IDX_HEADS * IDX_DIM + IDX_DIM + N_IDX_HEADS + SSM_WIDTH + CONV_DIM + N_SSM_HEADS
FFN_HIDDEN = -(-8 * D_MODEL // (3 * 256)) * 256
N_BUCKETS = 32
MAX_DISTANCE = 128
NORM_EPS = 1e-6
PROMPT_QBLOCK = 64
SAMPLE_QBLOCK = 1

kernel_name = "hymba_dsa_ssd_decoder_step"

def _split_points():
    sizes = [ATT_WIDTH, ATT_WIDTH, ATT_WIDTH, N_IDX_HEADS * IDX_DIM, IDX_DIM, N_IDX_HEADS,
             SSM_WIDTH, CONV_DIM, N_SSM_HEADS]
    return [int(s) for s in np.cumsum(sizes)[:-1]]

def rmsnorm(x, g):
    xf = x.astype(jnp.float32)
    y = xf * lax.rsqrt(jnp.mean(xf * xf, axis=-1, keepdims=True) + NORM_EPS)
    return (y * g.astype(jnp.float32)).astype(x.dtype)

def t5_bucket(rel):
    max_exact = N_BUCKETS // 2
    relf = jnp.maximum(rel, 1).astype(jnp.float32)
    large = max_exact + (jnp.log(relf / max_exact) / math.log(MAX_DISTANCE / max_exact)
                         * (N_BUCKETS - max_exact)).astype(jnp.int32)
    large = jnp.minimum(large, N_BUCKETS - 1)
    return jnp.where(rel < max_exact, rel, large)

def indexer_topk(qi, w, kidx, qpos, topk):
    s = jax.nn.relu(jnp.einsum('bqhd,bld->bqhl', qi, kidx))
    score = jnp.einsum('bqhl,bqh->bql', s, w).astype(jnp.float32)
    allowed = jnp.arange(kidx.shape[1], dtype=jnp.int32)[None, :] <= qpos[:, None]
    score = jnp.where(allowed[None], score, -jnp.inf)
    _, idx = lax.top_k(score, topk)
    return idx

def sparse_attend(q, k_sel, v_sel, idx, qpos, rel_bias):
    logits = jnp.einsum('bqhd,bqkhd->bqhk', q, k_sel).astype(jnp.float32) * (ATT_HEAD_DIM ** -0.5)
    rel = qpos[None, :, None] - idx
    bias = rel_bias[t5_bucket(jnp.maximum(rel, 0))]
    logits = logits + jnp.moveaxis(bias, -1, 2).astype(jnp.float32)
    logits = jnp.where((rel >= 0)[:, :, None, :], logits, -jnp.inf)
    p = jax.nn.softmax(logits, axis=-1)
    return jnp.einsum('bqhk,bqkhd->bqhd', p.astype(v_sel.dtype), v_sel)

def _gather_rows(a, i):
    return jax.vmap(lambda ab, ib: ab[ib])(a, i)

def dsa_prompt(q, k, v, qi, w, kidx, rel_bias):
    B, S = q.shape[:2]
    topk = min(TOPK_MAX, S // 4)
    nb = S // PROMPT_QBLOCK

    def blk(xs):
        qb, qib, wb, qpos = xs
        idx = indexer_topk(qib, wb, kidx, qpos, topk)
        return sparse_attend(qb, _gather_rows(k, idx), _gather_rows(v, idx), idx, qpos, rel_bias)

    to_blocks = lambda a: jnp.moveaxis(a.reshape(B, nb, PROMPT_QBLOCK, *a.shape[2:]), 1, 0)
    qpos = jnp.arange(S, dtype=jnp.int32).reshape(nb, PROMPT_QBLOCK)
    out = lax.map(blk, (to_blocks(q), to_blocks(qi), to_blocks(w), qpos))
    return jnp.moveaxis(out, 0, 1).reshape(B, S, ATT_WIDTH)

def dsa_sample(q, k_new, v_new, qi, w, kidx_new, cache_k, cache_v, cache_kidx, page_table, rel_bias):
    B, T = q.shape[:2]
    n_pages = page_table.shape[1]
    past = n_pages * PAGE_SIZE
    kidx_past = cache_kidx[page_table].reshape(B, past, IDX_DIM)
    kidx_all = jnp.concatenate([kidx_past, kidx_new], axis=1)
    topk = min(TOPK_MAX, (past + T) // 4)

    def gather(cache, new, idx):
        in_past = idx < past
        pidx = jnp.minimum(idx, past - 1)
        phys = jnp.take_along_axis(page_table, (pidx // PAGE_SIZE).reshape(B, -1), axis=1).reshape(idx.shape)
        rows_past = cache[phys, pidx % PAGE_SIZE]
        rows_new = _gather_rows(new, jnp.clip(idx - past, 0, T - 1))
        return jnp.where(in_past[..., None, None], rows_past, rows_new)

    nb = T // SAMPLE_QBLOCK

    def blk(xs):
        qb, qib, wb, qpos = xs
        idx = indexer_topk(qib, wb, kidx_all, qpos, topk)
        return sparse_attend(qb, gather(cache_k, k_new, idx), gather(cache_v, v_new, idx), idx, qpos, rel_bias)

    to_blocks = lambda a: jnp.moveaxis(a.reshape(B, nb, SAMPLE_QBLOCK, *a.shape[2:]), 1, 0)
    qpos = (past + jnp.arange(T, dtype=jnp.int32)).reshape(nb, SAMPLE_QBLOCK)
    out = lax.map(blk, (to_blocks(q), to_blocks(qi), to_blocks(w), qpos))
    return jnp.moveaxis(out, 0, 1).reshape(B, T, ATT_WIDTH)

def causal_conv(xbc, conv_w, conv_b, prefix):
    T = xbc.shape[1]
    xp = jnp.concatenate([prefix.astype(xbc.dtype), xbc], axis=1)
    out = conv_b + sum(xp[:, j:j + T] * conv_w[j] for j in range(CONV_W))
    return jax.nn.silu(out), xp[:, -(CONV_W - 1):]

def ssd_scan(x, dt, A, Bm, Cm, h0, chunk):
    Bsz, T = x.shape[:2]
    nc = T // chunk
    rep = N_SSM_HEADS // N_SSM_GROUPS
    f32 = jnp.float32
    Bh = jnp.repeat(Bm.astype(f32), rep, axis=2)
    Ch = jnp.repeat(Cm.astype(f32), rep, axis=2)
    a = dt * A
    to_chunks = lambda t: jnp.moveaxis(t.reshape(Bsz, nc, chunk, *t.shape[2:]), 1, 0)
    causal = jnp.tril(jnp.ones((chunk, chunk), dtype=bool))

    def step(h, xs):
        xc, dtc, ac, Bc, Cc = xs
        acum = jnp.cumsum(ac, axis=1)
        seg = acum[:, :, None, :] - acum[:, None, :, :]
        decay = jnp.exp(jnp.where(causal[None, :, :, None], seg, -jnp.inf))
        cb = jnp.einsum('bihn,bjhn->bijh', Cc, Bc)
        y_intra = jnp.einsum('bijh,bjh,bjhp->bihp', cb * decay, dtc, xc)
        y_inter = jnp.einsum('bihn,bhpn->bihp', Cc, h) * jnp.exp(acum)[..., None]
        last = acum[:, -1]
        wts = jnp.exp(last[:, None, :] - acum) * dtc
        h_new = h * jnp.exp(last)[..., None, None] + jnp.einsum('bjh,bjhn,bjhp->bhpn', wts, Bc, xc)
        return h_new, y_intra + y_inter

    h_fin, ys = lax.scan(step, h0.astype(f32),
                         (to_chunks(x.astype(f32)), to_chunks(dt), to_chunks(a), to_chunks(Bh), to_chunks(Ch)))
    y = jnp.moveaxis(ys, 0, 1).reshape(Bsz, T, N_SSM_HEADS, SSM_HEAD_DIM)
    return y, h_fin

def layer(x, att_fn, conv_prefix, h0, chunk, norm_attn, w_in, idx_k_norm, conv_w, conv_b,
          dt_bias, a_log, d_skip, ssm_norm, w_out, norm_ffn, w_gate, w_up, w_down):
    B, T, _ = x.shape
    u = rmsnorm(x, norm_attn)
    proj = u @ w_in
    q, k, v, qi, ki, wi, z, xbc, dtr = jnp.split(proj, _split_points(), axis=-1)
    q = q.reshape(B, T, N_ATT_HEADS, ATT_HEAD_DIM)
    k = k.reshape(B, T, N_ATT_HEADS, ATT_HEAD_DIM)
    v = v.reshape(B, T, N_ATT_HEADS, ATT_HEAD_DIM)
    qi = qi.reshape(B, T, N_IDX_HEADS, IDX_DIM)
    ki = rmsnorm(ki, idx_k_norm)
    att = att_fn(q, k, v, qi, wi, ki)

    xc, conv_tail = causal_conv(xbc, conv_w, conv_b, conv_prefix)
    xs = xc[..., :SSM_WIDTH].reshape(B, T, N_SSM_HEADS, SSM_HEAD_DIM)
    Bm = xc[..., SSM_WIDTH:SSM_WIDTH + N_SSM_GROUPS * SSM_STATE].reshape(B, T, N_SSM_GROUPS, SSM_STATE)
    Cm = xc[..., SSM_WIDTH + N_SSM_GROUPS * SSM_STATE:].reshape(B, T, N_SSM_GROUPS, SSM_STATE)
    dt = jax.nn.softplus(dtr.astype(jnp.float32) + dt_bias.astype(jnp.float32))
    A = -jnp.exp(a_log.astype(jnp.float32))
    y, h_fin = ssd_scan(xs, dt, A, Bm, Cm, h0, chunk)
    y = (y + d_skip.astype(jnp.float32)[:, None] * xs.astype(jnp.float32)).astype(x.dtype)
    y = rmsnorm(y.reshape(B, T, SSM_WIDTH) * jax.nn.silu(z), ssm_norm)

    h = x + jnp.concatenate([att, y], axis=-1) @ w_out
    f = rmsnorm(h, norm_ffn)
    h = h + (jax.nn.silu(f @ w_gate) * (f @ w_up)) @ w_down
    return h, k, v, ki, conv_tail, h_fin.astype(h0.dtype)

def setup_inputs(seed: int = 0) -> dict:
    key = jax.random.key(seed)
    ks = jax.random.split(key, 24)
    f32 = jnp.float32
    n_pages = PAST_LEN // PAGE_SIZE
    used = DEC_BATCH * n_pages
    n_phys = used + max(1, used // 4)
    nrm = lambda k, shape, s: s * jax.random.normal(k, shape, f32)
    dt0 = jnp.exp(jax.random.uniform(ks[14], (DEPTH, N_SSM_HEADS), f32, math.log(1e-3), math.log(1e-1)))
    return {
        "x_prompt": nrm(ks[0], (BATCH, SEQ, D_MODEL), 1.0),
        "x_sample": nrm(ks[1], (DEC_BATCH, DEC_SEQ, D_MODEL), 1.0),
        "cache_k": nrm(ks[2], (DEPTH, n_phys, PAGE_SIZE, N_ATT_HEADS, ATT_HEAD_DIM), 1.0),
        "cache_v": nrm(ks[3], (DEPTH, n_phys, PAGE_SIZE, N_ATT_HEADS, ATT_HEAD_DIM), 1.0),
        "cache_kidx": nrm(ks[4], (DEPTH, n_phys, PAGE_SIZE, IDX_DIM), 1.0),
        "state_conv": nrm(ks[5], (DEPTH, DEC_BATCH, CONV_W - 1, CONV_DIM), 1.0),
        "state_ssm": nrm(ks[6], (DEPTH, DEC_BATCH, N_SSM_HEADS, SSM_HEAD_DIM, SSM_STATE), 0.1),
        "page_table": jax.random.permutation(ks[7], n_phys)[:used].reshape(DEC_BATCH, n_pages).astype(jnp.int32),
        "rel_bias": nrm(ks[8], (N_BUCKETS, N_ATT_HEADS), 0.5),
        "norm_attn": 1.0 + nrm(ks[9], (DEPTH, D_MODEL), 0.02),
        "w_in": nrm(ks[10], (DEPTH, D_MODEL, IN_WIDTH), D_MODEL ** -0.5),
        "idx_k_norm": 1.0 + nrm(ks[11], (DEPTH, IDX_DIM), 0.02),
        "conv_w": nrm(ks[12], (DEPTH, CONV_W, CONV_DIM), CONV_W ** -0.5),
        "conv_b": nrm(ks[13], (DEPTH, CONV_DIM), 0.02),
        "dt_bias": dt0 + jnp.log(-jnp.expm1(-dt0)),
        "a_log": jnp.log(jax.random.uniform(ks[15], (DEPTH, N_SSM_HEADS), f32, 1.0, 16.0)),
        "d_skip": 1.0 + nrm(ks[16], (DEPTH, N_SSM_HEADS), 0.1),
        "ssm_norm": 1.0 + nrm(ks[17], (DEPTH, SSM_WIDTH), 0.02),
        "w_out": nrm(ks[18], (DEPTH, MIX_WIDTH, D_MODEL), MIX_WIDTH ** -0.5),
        "norm_ffn": 1.0 + nrm(ks[19], (DEPTH, D_MODEL), 0.02),
        "w_gate": nrm(ks[20], (DEPTH, D_MODEL, FFN_HIDDEN), D_MODEL ** -0.5),
        "w_up": nrm(ks[21], (DEPTH, D_MODEL, FFN_HIDDEN), D_MODEL ** -0.5),
        "w_down": nrm(ks[22], (DEPTH, FFN_HIDDEN, D_MODEL), FFN_HIDDEN ** -0.5),
        "norm_final": 1.0 + nrm(ks[23], (D_MODEL,), 0.02),
    }

def reference(x_prompt, x_sample, cache_k, cache_v, cache_kidx, state_conv, state_ssm, page_table,
              rel_bias, norm_attn, w_in, idx_k_norm, conv_w, conv_b, dt_bias, a_log, d_skip, ssm_norm,
              w_out, norm_ffn, w_gate, w_up, w_down, norm_final):
    hp, hs = x_prompt, x_sample
    kp, vp, kip, cp, sp = [], [], [], [], []
    ksm, vsm, kism, csm, ssm_s = [], [], [], [], []
    zero_conv = jnp.zeros((x_prompt.shape[0], CONV_W - 1, CONV_DIM), x_prompt.dtype)
    zero_ssm = jnp.zeros((x_prompt.shape[0], N_SSM_HEADS, SSM_HEAD_DIM, SSM_STATE), state_ssm.dtype)
    for l in range(DEPTH):
        wl = (norm_attn[l], w_in[l], idx_k_norm[l], conv_w[l], conv_b[l], dt_bias[l], a_log[l],
              d_skip[l], ssm_norm[l], w_out[l], norm_ffn[l], w_gate[l], w_up[l], w_down[l])
        att_p = lambda q, k, v, qi, wi, ki: dsa_prompt(q, k, v, qi, wi, ki, rel_bias)
        hp, k1, v1, ki1, c1, s1 = layer(hp, att_p, zero_conv, zero_ssm, SSD_CHUNK, *wl)
        ck, cv, cki = cache_k[l], cache_v[l], cache_kidx[l]
        att_s = lambda q, k, v, qi, wi, ki: dsa_sample(q, k, v, qi, wi, ki, ck, cv, cki, page_table, rel_bias)
        hs, k2, v2, ki2, c2, s2 = layer(hs, att_s, state_conv[l], state_ssm[l], hs.shape[1], *wl)
        kp.append(k1); vp.append(v1); kip.append(ki1); cp.append(c1); sp.append(s1)
        ksm.append(k2); vsm.append(v2); kism.append(ki2); csm.append(c2); ssm_s.append(s2)
    y_prompt = rmsnorm(hp, norm_final)
    y_sample = rmsnorm(hs, norm_final)
    return (y_prompt, y_sample,
            jnp.stack(kp), jnp.stack(vp), jnp.stack(kip), jnp.stack(cp), jnp.stack(sp),
            jnp.stack(ksm), jnp.stack(vsm), jnp.stack(kism), jnp.stack(csm), jnp.stack(ssm_s))


_drawn_inputs = setup_inputs


def setup_inputs(seed=0):
    import zlib

    import numpy as np

    out = dict(_drawn_inputs(seed))
    spreads = {}
    factors = {'idx_k_norm': 7.59,
     'ssm_norm': 4.72,
     'norm_ffn': 4.594,
     'norm_final': 8.25,
     'rel_bias': 3.072}
    for name, (base, spread) in spreads.items():
        noise = np.random.default_rng([zlib.crc32(name.encode()), seed]).standard_normal(out[name].shape)
        drawn = base * np.exp(spread * noise) if base else spread * noise
        out[name] = __import__('jax').numpy.asarray(drawn.astype(out[name].dtype))
    for name, factor in factors.items():
        out[name] = (out[name] * factor).astype(out[name].dtype)
    return out
```

```python
import math
import numpy as np
import concourse.bass as bass
from concourse import mybir
from contextlib import ExitStack

F32 = mybir.dt.float32
F32R = mybir.dt.float32r
I32 = mybir.dt.int32
ALU = mybir.AluOpType
ACT = mybir.ActivationFunctionType
AX = mybir.AxisListType

P = 128
DM = 2048
KT = DM // P
NP, NB, NQ = 512, 8, 8
NS = NB * NQ
NT = NP + NS
HALF = NT // 2
NH, DH = 8, 128
NI, DI = 16, 64
NM, DS = 16, 64
CONV = 1536
QKV, QI0, KI0, Z0, XB0, DT0 = 1024, 3072, 4096, 4176, 5200, 6736
HID = 5632
NG = HID // 512
PAST, PAGE = 512, 128
TOPK_P, TOPK_S = 128, 130
MASKED = -3.0e38
BIG = 1.0e30
REL = 384
SCALE = DH ** -0.5
EPS = 1e-6


def build(nc, I, O):
    ctx = ExitStack()
    with ctx:
        base = (nc.sbuf_base + 31) // 32 * 32
        top = [base]

        def sb(name, shape, dt=F32, at=None):
            size = (int(np.prod(shape[1:])) * 4 + 31) // 32 * 32
            if at is None:
                at = top[0]
                top[0] += size
            assert at + size <= nc.sbuf_usable_end, (name, at + size - nc.sbuf_usable_end)
            spot[name] = at, at + size
            return nc.alloc_sbuf_tensor_at(name, shape, dt, offset=at)

        spot = {}

        def sem(name):
            return ctx.enter_context(nc.semaphore(name))

        def scratch(name, shape):
            return nc.dram_tensor(name, shape, F32).ap()

        AH = sb("AH", [P, KT, NT], F32R)
        AL = sb("AL", [P, KT, NT], F32R)
        WRAW = sb("WRAW", [P, 4, KT * P])
        WH = sb("WH", [P, 2, 8, P], F32R)
        WL = sb("WL", [P, 2, 8, P], F32R)
        ident = sb("ident", [P, P])
        ones = sb("ones", [P, P])
        eps = sb("eps", [P, 1])
        g_attn = sb("g_attn", [P, KT])
        rstd = sb("rstd", [P, 2, HALF])
        tokd = sb("tokd", [P, 5, 3, NM])
        neg_p = sb("neg_p", [P, 1280])
        neg_s = sb("neg_s", [NS, NT])
        page = sb("page", [1, 32], I32)
        gains = sb("gains", [P, 40])
        side = top[0]
        PT_OFF = [0, 128, 384, 768]

        XR = sb("XR", [P, KT, NT], at=side)
        xin = sb("xin", [P, 4, DM], at=spot["XR"][1])
        sq = sb("sq", [P, 3, NT], at=spot["neg_p"][0])
        sqsum = sb("sqsum", [P, NT], at=spot["xin"][1] - NT * 4)

        top[0] = side
        qi2 = sb("qi2", [P, NI // 2, NT])
        qis = sb("qis", [DI, NB, NI, NQ])
        kwd = sb("kwd", [112, NT])
        kwt = sb("kwt", [P, 5, 112])
        kin = sb("kin", [P, 5, 2, DI])
        kit = sb("kit", [P, NT])
        kc = sb("kc", [P, 4, 4, DI])
        kcT = sb("kcT", [DI, 2, PAST])
        wsel = sb("wsel", [P, NB, NS])
        selm = sb("selm", [P, NB, NS])
        sc = sb("sc", [P, 1152])
        scs = sb("scs", [NS, NT])
        da = sb("da", [NM, 3, NT], at=spot["sc"][0])
        rl = sb("rl", [P, 4, 512])
        dtmp = sb("dtmp", [NM, 4, NT], at=spot["rl"][0])
        top[0] = max(top[0], spot["dtmp"][1])
        cb = sb("cb", [P, 2, 3 + NP])
        cs = sb("cs", [P, 2, NB, 3 + NQ])
        ev = sb("ev", [P, 2, 2, HALF])
        qtmp = sb("qtmp", [DI, NI // 2, NS], at=spot["cb"][0])
        stc = sb("stc", [24, CONV], at=spot["cb"][0])
        tails = sb("tails", [P, 12, 27])
        sct = sb("sct", [P, 12, 24])
        wtok = sb("wtok", [P, 5, NI])
        wcol = sb("wcol", [P, NB])
        small = sb("small", [P, 160])
        gk = sb("gk", [P, DI])
        dvec = sb("dvec", [NM, 4])
        convw = sb("convw", [P, 12, 5])
        rbt = sb("rbt", [32, NH])
        oh = sb("oh", [32, REL])
        bdt = sb("bdt", [NH, REL])
        smask = sb("smask", [NS, NS])
        dmask = sb("dmask", [P, P])
        tailT = sb("tailT", [27, CONV], at=spot["qi2"][0])
        work = sb("work", [P, NT], at=spot["tailT"][1])
        eqt = sb("eqt", [P, NT], at=spot["work"][1])
        gtt = sb("gtt", [P, NT], at=spot["eqt"][1])
        cum = sb("cum", [P, NT], at=spot["qis"][0])

        top[0] = side
        raw3 = sb("raw3", [P, 3, 8, P], at=spot["WRAW"][0] + 16384)
        h0 = sb("h0", [P, NB, P], at=spot["raw3"][1])
        vca = sb("vca", [P, NB, 4, DH], at=spot["WRAW"][0])
        qT = sb("qT", [P, NT])
        kT = sb("kT", [P, NT])
        vT = sb("vT", [P, NT])
        qpad = sb("qpad", [P, NB, NS])
        bias_p = sb("bias_p", [P, 2 * P])
        bias_s = sb("bias_s", [NS, P + NQ])
        lg = sb("lg", [P, 1280])
        lgs = sb("lgs", [NS, NT])
        stat = sb("stat", [P, 3, 8])
        pt = sb("pt", [P, 2, NP])
        pts = sb("pts", [P, 5, NS])
        kca = sb("kca", [P, 2, 4, DH])
        kcaT = sb("kcaT", [P, 2, PAST])
        vtok = sb("vtok", [P, 5, DH])
        ktok = sb("ktok", [P, 5, DH])
        attT = sb("attT", [P, NT])
        xs = sb("xs", [P, NT])
        ssq = sb("ssq", [P, NT])
        bf = sb("bf", [P, NT])
        cf = sb("cf", [P, NT])
        ea = sb("ea", [P, NT])
        sz = sb("sz", [P, NT])
        abc = sb("abc", [P, 2, NT])
        xtok = sb("xtok", [P, 5, P])
        btok = sb("btok", [P, 5, P])
        xw = sb("xw", [P, 5, P])
        cbm = sb("cbm", [P, 5, P])
        ex = sb("ex", [P, 2, P])
        mt = sb("mt", [P, 4, P])
        hT = sb("hT", [P, 4, P])
        hTb = sb("hTb", [P, NB, P])
        fin = cbm[:, 0, :]
        colb = sb("colb", [P, 5, 3, 2])
        elt = sb("elt", [P, 2, 4])
        els = sb("els", [P, NB])
        dcol = sb("dcol", [P, 1])
        cmask = sb("cmask", [P, P], at=spot["ones"][0])
        bmask = sb("bmask", [NS, NS])
        own = sb("own", [NS, NB])
        bmask8 = own[:, :].rearrange("p (b n) -> p b n", n=1)

        mx = sb("mx", [P, 6, NT], at=spot["bf"][0])
        hh = sb("hh", [P, 4, NT], F32R, at=spot["attT"][1])
        hl = sb("hl", [P, 4, NT], F32R, at=spot["hh"][1])
        assert spot["attT"][1] >= side + KT * NT * 4
        top[0] = max(spot["hl"][1], spot["mx"][1])
        xt = sb("xt", [P, 2, NT])
        sqf = sb("sqf", [P, 2, NT])
        gs = sb("gs", [P, 2, NT])
        acc = gs[:, 0, :]
        us = sb("us", [P, 2, NT], at=spot["xt"][0])
        y_out = sb("y_out", [P, 4, DM], at=spot["AH"][0])
        y_outs = sb("y_outs", [NS, DM], at=spot["AL"][0])
        pick = sb("pick", [P, 9])
        rfin = sb("rfin", [P, 5])

        G = [ctx.enter_context(nc.psum_tensor(f"G{i}", [P, 2, 512], F32)) for i in range(2)]
        B = [ctx.enter_context(nc.psum_tensor(f"B{i}", [P, 512], F32)) for i in range(4)]

        xres = scratch("xres", (KT, P, NT))
        zS = scratch("zS", (8, P, NT))
        xcS = scratch("xcS", (12, P, NT))
        acS = scratch("acS", (NM, NT))
        wiS = scratch("wiS", (NI, NS))
        mixS = scratch("mixS", (KT, P, NT))
        bdS = scratch("bdS", (NH, REL))
        bdX = scratch("bdX", (NH, P, REL))

        names = """pick_done ry_done y_norm m_hi mix_lo sqf_done ssf_used f_hi f_lo g_silu h_mul hh_done hl_done d_tile o_sq
            o_scaled fss_used rfin_done y_scaled y_out bdx_out h_init h_in bias_in qpad_done lg_done nmax expd prob kout
            vout mixa vca_in kq ssm_in xw_done ea_done seg exd mt_done hT_done bblk h_done hout y_done ymix finout link_a
            link_s c_in x_store sq_A sq_D ss_done a_hi a_lo w_hi w_lo w_used tile_taken ki_ms ki_rt ki_n ki_out qis_done
            dt_in dt_a dt_b da_done da_st ac_out qis_in wi_out wcol_in wsel_done rl_used rls_used topk bd_out ev_silu
            cv_done cv_silu stc_in tail_out chain init""".split()
        s = {n: sem(n) for n in names}
        x_in = [sem(f"x_in{t}") for t in range(5)]
        w_in = [sem(f"w_in{t}") for t in range(2)]
        w_ld = [sem(f"w_ld{t}") for t in range(2)]
        mx_in = [sem(f"mx_in{t}") for t in range(6)]
        xt_in = [sem(f"xt_in{t}") for t in range(2)]
        r_in = [sem(f"r_in{t}") for t in range(3)]
        kca_in = [sem(f"kca_in{t}") for t in range(2)]
        kc_in = [sem(f"kc_in{t}") for t in range(4)]
        ev_st = [sem(f"ev_st{t}") for t in range(2)]
        full = [sem(f"full{b}") for b in range(4)]
        free = [sem(f"free{b}") for b in range(4)]
        block = ctx.enter_context(nc.Block())

        use = {}
        count = [0] * 4

        def plan(name, b):
            use[name] = b, count[b]
            count[b] += 1
        for n in range(20):
            plan(("x", n), n % 2)
        plan("ss0", 2)
        plan("ss1", 3)
        plan("bd", 0)
        for m in range(3):
            plan(("sct", m), 1)
        plan("kw0", 0)
        plan("kw1", 1)
        for j in range(3):
            plan(("tok", j), 2 + j % 2)
        plan("ki0", 0)
        plan("ki1", 1)
        plan("comb", 3)
        n = 0
        for hp in range(8):
            for t in (1, 2, 3):
                for e in range(2):
                    plan(("score", hp, t, e), e)
                    n += 1
            plan(("kcT", hp), 2)
            plan(("ss", hp), 2)
        plan("new0", 0)
        plan("new1", 1)
        for j in range(3):
            plan(("tail", j), j)

        turn = [("qk0", 0), ("qk1", 1), ("qk2", 0), ("qk3", 1), ("lnew", 0), ("xtok0", 2), ("xtok1", 3), ("btok0", 2), ("btok1", 3),
                ("ktok0", 1), ("ktok1", 0), ("cb0", 2), ("cb1", 3), ("kca0", 0), ("kca1", 1), ("su", 3), ("S", 2), ("kca2", 0), ("hTb0", 3),
                ("kca3", 1), ("y0", 3), ("kca4", 0), ("hTb1", 3), ("kca5", 1), ("y1", 3), ("vtok0", 0), ("vtok1", 1), ("y2", 3),
                ("kca6", 0), ("y3", 3), ("kca7", 1), ("pt0", 0), ("ys", 3), ("pt1", 0), ("pv0", 1), ("us0", 3), ("pt2", 0), ("pv1", 1), ("us1", 2),
                ("pt3", 0), ("pv2", 1), ("fin", 3), ("pv3", 1), ("pts", 0), ("pvs", 1)]
        MAMBA = {"xtok0", "xtok1", "btok0", "btok1", "cb0", "cb1", "su", "hTb0", "hTb1", "y0", "y1", "y2", "y3", "ys", "us0", "us1", "fin"}
        where = dict(turn)
        in_turn, in_mamba, in_att = {}, {}, {}
        n_all, n_mamba, n_att = [0] * 4, [0] * 4, [0] * 4
        for name, b in turn:
            in_turn[name] = n_all[b]
            n_all[b] += 1
            if name in MAMBA:
                in_mamba[name] = n_mamba[b]
                n_mamba[b] += 1
            else:
                in_att[name] = n_att[b]
                n_att[b] += 1

        def nth(name, i):
            b = where[name]
            if isinstance(i, int) and i == 0:
                return first[b] + in_mamba[name]
            if isinstance(i, int) and i == 8:
                return first[b] + n_mamba[b] + 7 * n_all[b] + extra[b] + in_att[name]
            return n_all[b] * i + (first[b] + n_mamba[b] - n_all[b] + in_turn[name])

        first, extra = list(count), [0, 0, 1, 1]
        for b in range(4):
            count[b] = first[b] + n_mamba[b] + 7 * n_all[b]
        plan("ssy0", 2)
        plan("ssy1", 3)
        for b in range(4):
            count[b] += n_att[b]
        plan("ssf0", 2)
        plan("ssf1", 3)
        plan("fss", 2)
        n = 0
        for m in range(4):
            for t in range(5):
                plan(("y", m, t), (0, 1, 3)[n % 3])
                n += 1

        def tclaim(eng, name, i):
            eng.wait_ge(free[where[name]], nth(name, i))

        def twait(eng, name, i):
            eng.wait_ge(full[where[name]], nth(name, i) + 1)

        def tgiven(eng, name, i):
            eng.wait_ge(free[where[name]], nth(name, i) + 1)

        def tmade(ins, name):
            ins.then_inc(full[where[name]], 1)

        def ttaken(ins, name):
            ins.then_inc(free[where[name]], 1)

        def bank(name):
            return B[use[name][0] if name in use else where[name]]

        def claim(eng, name):
            b, n = use[name]
            if n:
                eng.wait_ge(free[b], n)

        def made(ins, name):
            ins.then_inc(full[use[name][0]], 1)

        def wait(eng, name):
            b, n = use[name]
            eng.wait_ge(full[b], n + 1)

        def given(eng, name):
            b, n = use[name]
            eng.wait_ge(free[b], n + 1)

        def taken(ins, name):
            ins.then_inc(free[use[name][0]], 1)

        C3, T3 = 58 + 48, 29 + 24
        TF = T3 + KT
        D_AT = {1: 0, 2: 1}
        LOADS = 16 * 11
        NCONST = 2 + 9 + 4 + 2 + 3
        PAIR_COL = [QI0 + 256 * p for p in range(4)] + [Z0 + 256 * p for p in range(4)] + [XB0 + 256 * p for p in range(6)]
        w_v = I["w_in"].rearrange("(k p) n -> p k n", p=P)

        def y_tok(t):
            return y_out[:, t, :] if t < 4 else y_outs[:, :]

        @block.sync
        def _(sp):
            def const(dst, src, slow=False):
                sp.dma_start(dst, src, allow_slow_non_contiguous=slow).then_inc(s["c_in"], 16)
            for t in range(4):
                sp.dma_start(xin[:, t, :], I["x_prompt"][t * P:(t + 1) * P, :]).then_inc(x_in[t], 16)
            const(ident[:, :], I["ident"])
            const(g_attn[:, :], I["norm_attn"].rearrange("(k p) -> p k", p=P), True)
            sp.dma_start(WRAW[:, 0, :].rearrange("p (k c) -> p k c", c=P)[:, :, 0:96], w_v[:, :, KI0:KI0 + 96]).then_inc(w_in[0], 16)
            sp.dma_start(WRAW[:, 0, :].rearrange("p (k c) -> p k c", c=P)[:, :, 96:112], w_v[:, :, DT0:DT0 + 16]).then_inc(w_in[0], 16)

            def load_pair(p):
                if p >= 2:
                    sp.wait_ge(s["w_lo"], 4 * p - 6)
                dst = WRAW[:, 2 * (p % 2):2 * (p % 2) + 2, :].rearrange("p s (k c) -> p (s k c)", c=P).rearrange("p (k c) -> p k c", c=256)
                c = PAIR_COL[p - 1]
                sp.dma_start(dst, w_v[:, :, c:c + 256]).then_inc(w_in[p % 2], 16)
            load_pair(1)
            sp.wait_ge(full[1], 2)
            sp.dma_start(xin[0:NS, 0, :], I["x_sample"]).then_inc(x_in[4], 16)
            sp.wait_ge(free[0], 10)
            sp.wait_ge(free[1], 10)
            sp.dma_start(xres.rearrange("k p n -> p k n"), XR[:, :, :]).then_inc(s["x_store"], 16)
            load_pair(2)
            sp.wait_ge(s["a_lo"], KT)
            sp.wait_ge(s["a_hi"], KT)
            wait(sp, "ss0")
            wait(sp, "ss1")
            sp.wait_ge(s["x_store"], 16)
            const(oh[:, :], I["onehot"])
            const(rbt[:, :], I["rel_bias"])
            const(gk[:, :], I["idx_k_norm"].partition_broadcast(P))
            const(selm[:, :, :], I["select_row"])
            const(smask[:, :], I["decode_mask"])
            const(dmask[:, :], I["causal_score"])
            const(neg_p[:, 0:P], I["causal_logit"])
            const(dvec[:, 0:1], I["dt_bias"].rearrange("(h a) -> h a", a=1), True)
            const(dvec[:, 1:2], I["a_log"].rearrange("(h a) -> h a", a=1), True)
            for j in range(4):
                const(convw[:, :, j], I["conv_w"][j, :].rearrange("(m p) -> p m", p=P), True)
            const(convw[:, :, 4], I["conv_b"].rearrange("(m p) -> p m", p=P), True)
            const(gains[:, 0:16], I["norm_ffn"].rearrange("(k p) -> p k", p=P), True)
            const(gains[:, 16:32], I["norm_final"].rearrange("(k p) -> p k", p=P), True)
            const(gains[:, 32:40], I["ssm_norm"].rearrange("(k p) -> p k", p=P), True)
            const(page[:, :], I["page_table"].rearrange("(a b) -> a b", a=1))
            sp.dma_start(stc[:, :], I["state_conv"]).then_inc(s["stc_in"], 16)
            sp.wait_ge(s["c_in"], 16 * NCONST)

            def phys(b, j):
                n = 4 * b + j
                return sp.value_load(page[0:1, n:n + 1], min_val=0, max_val=I["cache_kidx"].shape[0] // PAGE - 1) * PAGE

            def load_kc(b):
                if b >= 4:
                    sp.wait_ge(full[2], use[("kcT", b - 4)][1] + 1)
                for j in range(4):
                    sp.dma_start(kc[:, b % 4, j, :], I["cache_kidx"][bass.ds(phys(b, j), PAGE), :]).then_inc(kc_in[b % 4], 16)
            sp.wait_ge(s["tile_taken"], 1)
            sp.dma_start(dtmp[:, 0, :], kwd[96:112, :]).then_inc(s["dt_in"], 16)
            sp.dma_start(wiS, kwd[64:80, NP:NT]).then_inc(s["wi_out"], 16)
            sp.wait_ge(s["wi_out"], 16)
            for b in range(NB):
                sp.dma_start(wcol[:, b:b + 1], bass.AP(wiS.tensor, b * NQ, [[NS, NI], [1, NQ], [1, 1]]), allow_slow_non_contiguous=True).then_inc(s["wcol_in"], 16)
            load_pair(3)
            for b in range(4):
                load_kc(b)
            sp.wait_ge(s["ki_n"], 1)
            sp.dma_start(O["kidx_prompt"].rearrange("(t p) d -> p t d", p=P), kin[:, 0:4, 0, :]).then_inc(s["ki_out"], 16)
            sp.dma_start(O["kidx_sample"], kin[0:NS, 4, 0, :]).then_inc(s["ki_out"], 16)
            given(sp, "bd")
            sp.dma_start(bdS, bdt[:, :]).then_inc(s["bd_out"], 16)
            sp.wait_ge(s["bd_out"], 16)
            sp.dma_start(bdX, bass.AP(bdS.tensor, 0, [[REL, NH], [0, P], [1, REL]])).then_inc(s["bdx_out"], 16)
            sp.wait_ge(s["da_done"], 1)
            sp.dma_start(acS, da[:, 1, :]).then_inc(s["ac_out"], 16)
            for p in range(4, 15):
                if p == 6:
                    sp.wait_ge(s["tile_taken"], 9)
                    given(sp, ("sct", 2))
                    sp.dma_start(qtmp[:, :, :], qi2[DI:P, :, NP:NT]).then_inc(s["qis_in"], 16)
                load_pair(p)
                for b in {7: (4,), 8: (5, 6), 9: (7,)}.get(p, ()):
                    load_kc(b)
            def load_half(i, n):
                sp.wait_ge(s["w_lo"], 6 * i + (54 if isinstance(i, int) and i == 0 and n < 3 else 56 + n))
                sp.dma_start(raw3[:, n % 3, :, :], w_v[:, 8 * (n % 2):8 * (n % 2) + 8, bass.ds(i * P + QKV * (n // 2), P)]).then_inc(r_in[n % 3], 16)
            for n in range(4):
                load_half(0, n)
            first_pages = [[phys(b, j) for j in range(4)] for b in range(4)]

            for g in range(3):
                given(sp, ("tail", g))
            sp.wait_ge(s["bd_out"], 16)
            sp.dma_start(O["conv_prompt"], tailT[0:3, :]).then_inc(s["tail_out"], 16)
            sp.dma_start(O["conv_sample"], tailT[3:27, :]).then_inc(s["tail_out"], 16)
            sp.wait_ge(s["topk"], 4)
            sp.wait_ge(s["cv_silu"], 12)
            sp.wait_ge(s["tail_out"], 32)
            sp.wait_ge(s["bdx_out"], 16)
            sp.wait_ge(s["ki_out"], 32)
            for m in range(2):
                sp.wait_ge(ev_st[m], 160)
            sp.dma_start(cmask[:, :], I["causal_T"]).then_inc(s["h_in"], 16)
            sp.dma_start(bmask[:, :], I["decode_T"]).then_inc(s["h_in"], 16)
            sp.dma_start(own[:, :], I["own_sequence"]).then_inc(s["h_in"], 16)

            def load_mamba(i):
                one = lambda ap: ap.then_inc(s["ssm_in"], 16)
                rows = lambda t, n: bass.AP(t.tensor, n * (P * NT), [[NT, P], [1, NT]])
                one(sp.dma_start(xs[:, :], rows(xcS, i)))
                one(sp.dma_start(bf[:, :], rows(xcS, i // 4 + 8)))
                one(sp.dma_start(cf[:, :], rows(xcS, i // 4 + 10)))
                one(sp.dma_start(sz[:, :], rows(zS, i)))
                for e in range(2):
                    one(sp.dma_start(ea[e * DS:(e + 1) * DS, :], bass.AP(acS.tensor, i * (2 * NT) + e * NT, [[0, DS], [1, NT]])))
                    one(sp.dma_start(abc[:, e, :], bass.AP(acS.tensor, i * (2 * NT) + e * NT, [[0, P], [1, NT]])))
                    one(sp.dma_start(dcol[e * DS:(e + 1) * DS, :], bass.AP(I["d_skip"].tensor, i * 2 + e, [[0, DS], [1, 1]])))
                one(sp.dma_start(h0[:, :, :], bass.AP(I["state_ssm"].tensor, i * (P * P), [[P, P], [NM * DS * P, NB], [1, P]])))

            def load_bias(a):
                if not (isinstance(a, int) and a == 0):
                    sp.wait_ge(s["lg_done"], 5 * a)
                sp.dma_start(bias_p[:, :], bass.AP(bdX.tensor, a * (P * REL) + P - 1, [[REL - 1, P], [1, 2 * P]])).then_inc(s["bias_in"], 16)
                sp.dma_start(bias_s[:, :], bass.AP(bdX.tensor, a * (P * REL) + P - 1, [[0, NB], [REL - 1, NQ], [1, P + NQ]])).then_inc(s["bias_in"], 16)

            def load_k(a, b, rows, i=None):
                if i is not None:
                    twait(sp, f"kca{(b - 2) % NB}", i)
                for j in range(4):
                    sp.dma_start(kca[:, b % 2, j, :], I["cache_k"][bass.ds(rows[j], PAGE), bass.ds(a * DH, DH)]).then_inc(kca_in[b % 2], 16)

            def load_v(a, b, rows):
                for j in range(4):
                    sp.dma_start(vca[:, b, j, :], I["cache_v"][bass.ds(rows[j], PAGE), bass.ds(a * DH, DH)]).then_inc(s["vca_in"], 16)

            def turn_sp(i, att=True, units=True, mamba=True, more=True):
                a = i - 1
                if att:
                    load_bias(a)
                for n in range(6):
                    if units and (more or n < 3) and not (n < 3 and isinstance(i, int) and i == 0):
                        load_half(i if n < 3 else i + 1, (n + 3) % 6)
                    if n < 2 and att:
                        if n == 0 and not (isinstance(a, int) and a == 0):
                            twait(sp, "pvs", a)
                        for b in (2 * n, 2 * n + 1):
                            load_v(a, b, first_pages[b])
                    if n == 3 and att:
                        for b in (2, 3):
                            load_k(a, b, first_pages[b], i)
                    if n >= 4 and att:
                        two = (2 * n - 4, 2 * n - 3)
                        rows = [[phys(b, j) for j in range(4)] for b in two]
                        for b, r in zip(two, rows):
                            load_k(a, b, r, i)
                        for b, r in zip(two, rows):
                            load_v(a, b, r)
                    if n == 5 and mamba:
                        twait(sp, "ys", i)
                        sp.wait_ge(s["ymix"], 16 * i + 16)
                        sp.wait_ge(s["hout"], 16 * i + 16)
                        sp.wait_ge(s["link_s"], 4 * i + 4)
                        load_mamba(i + 1)
                    if n == 5 and att and units:
                        for b in range(2):
                            load_k(a + 1, b, first_pages[b], i)
            load_mamba(0)
            load_half(0, 4)
            load_half(0, 5)
            sp.wait_ge(s["w_lo"], 58)
            for b in range(2):
                load_k(0, b, first_pages[b])
            turn_sp(0, att=False)
            turn_sp(1)
            with sp.Fori(2, 7) as i:
                turn_sp(i)
            turn_sp(7, mamba=False, more=False)
            turn_sp(8, units=False, mamba=False)

            wo_v = I["w_out"].rearrange("(k p) n -> p k n", p=P)

            def load_w(q, src, f):
                slot = (2, 0)[f % 2]
                if not (isinstance(q, int) and q < 2):
                    sp.wait_ge(s["w_lo"], 4 * q + (C3 - 4))
                dst = WRAW[:, slot:slot + 2, :].rearrange("p s c -> p (s c)")
                for d, a in src(dst):
                    sp.dma_start(d, a).then_inc(w_ld[f % 2], 32 // len(src(dst)))

            def out_cols(q):
                def src(dst):
                    d = dst.rearrange("p (k c) -> p k c", c=256)
                    return [(d[:, 8 * h:8 * h + 8, :], wo_v[:, 8 - 8 * h:16 - 8 * h, 256 * q:256 * q + 256]) for h in range(2)]
                return src

            def load_mix(j):
                if j >= 6:
                    sp.wait_ge(s["mix_lo"], j - 5)
                if j == 15:
                    sp.wait_ge(s["mixa"], 16 * NH)
                sp.dma_start(mx[:, j % 6, :], mixS[(j + 8) % KT]).then_inc(mx_in[j % 6], 16)

            def load_x(n):
                if n >= 2:
                    sp.wait_ge(s["tile_taken"], T3 + n - 1)
                sp.dma_start(xt[:, n % 2, :], xres[n]).then_inc(xt_in[n % 2], 16)
            sp.wait_ge(s["w_lo"], C3)
            sp.wait_ge(s["hout"], 16 * 8)
            load_w(0, out_cols(0), 0)
            sp.wait_ge(s["ymix"], 16 * 8)
            sp.wait_ge(s["finout"], 16 * 8)
            sp.wait_ge(s["h_done"], 16)
            sp.wait_ge(s["link_s"], 4 * 8)
            sp.wait_ge(s["mixa"], 16 * 7)
            for j in range(6):
                load_mix(j)
            twait(sp, "pvs", 8)
            load_w(1, out_cols(1), 1)
            sp.wait_ge(s["kout"], 32 * NH)
            sp.wait_ge(s["vout"], 32 * NH)
            load_x(0)
            load_x(1)
            for j in range(6, KT):
                load_mix(j)
            for q in range(2, 8):
                load_w(q, out_cols(q), q)
                load_x(2 * q - 2)
                load_x(2 * q - 1)
            def columns(w, c):
                v = I[w].rearrange("(k p) n -> p k n", p=P)
                return lambda dst: [(dst.rearrange("p (k c) -> p k c", c=256), v[:, :, bass.ds(c, 256)])]

            def down_rows(g, half):
                return lambda dst: [(dst.rearrange("p (k c) -> p k c", c=1024), bass.AP(I["w_down"].tensor, g * (4 * P * DM) + 1024 * half, [[DM, P], [P * DM, 4], [1, 1024]]))]

            load_w(8, columns("w_gate", 0), 0)
            load_x(14)
            load_x(15)
            load_w(9, columns("w_up", 0), 1)
            load_w(10, columns("w_gate", 256), 0)
            load_w(11, columns("w_up", 256), 1)
            with sp.Fori(1, NG) as g:
                q = 6 * g + 6
                load_w(q, columns("w_gate", g * 512), 0)
                load_w(q + 1, down_rows(g - 1, 0), 1)
                load_w(q + 2, down_rows(g - 1, 1), 0)
                load_w(q + 3, columns("w_up", g * 512), 1)
                load_w(q + 4, columns("w_gate", g * 512 + 256), 0)
                load_w(q + 5, columns("w_up", g * 512 + 256), 1)
            for d in range(2):
                load_w(6 * NG + 6 + d, down_rows(NG - 1, d), d)
            sp.wait_ge(s["tail_out"], 32)
            for t in range(5):
                sp.wait_ge(s["y_scaled"], t + 1)
                src = y_tok(t)
                sp.dma_start(O["y_prompt"][t * P:(t + 1) * P, :] if t < 4 else O["y_sample"], src).then_inc(s["y_out"], 16)
            sp.wait_ge(s["y_out"], 80)

        def upper(act, c, raw, half, w=P):
            if not (isinstance(c, int) and c < 2):
                act.wait_ge(s["w_used"], c - 1)
            nc.scalar.copy(WH[:, half, :, 0:w], raw[:, 8 * half:8 * half + 8, :]).then_inc(s["w_hi"], 1)

        def lower(pool, c, raw, half, w=P):
            pool.wait_ge(s["w_hi"], c + 1)
            nc.gpsimd.tensor_tensor(WL[:, half, :, 0:w], raw[:, 8 * half:8 * half + 8, :], WH[:, half, :, 0:w].bitcast(F32), ALU.subtract).then_inc(s["w_lo"], 1)

        def w_down_half(pslot, h):
            return WRAW[:, 2 * pslot:2 * pslot + 2, :].rearrange("p s c -> p (s c)").rearrange("p (k c) -> p k c", c=1024)[:, :, 256 * h:256 * h + 256]

        def as_down(w, half):
            return w[:, half, :, :].rearrange("p (k t) c -> p k (t c)", t=2)

        def upper_p(act, c, h, f, down):
            act.wait_ge(s["w_used"], c - 1)
            if down:
                nc.scalar.copy(as_down(WH, h % 2), w_down_half((1, 0)[f % 2], h)).then_inc(s["w_hi"], 1)
            else:
                nc.scalar.copy(WH[:, h % 2, :, :], raw_pair((1, 0)[f % 2], h // 2)[:, 8 * (h % 2):8 * (h % 2) + 8, :]).then_inc(s["w_hi"], 1)

        def lower_p(pool, c, h, f, down):
            pool.wait_ge(s["w_hi"], c + 1)
            if down:
                nc.gpsimd.tensor_tensor(as_down(WL, h % 2), w_down_half((1, 0)[f % 2], h), as_down(WH, h % 2).bitcast(F32), ALU.subtract).then_inc(s["w_lo"], 1)
            else:
                nc.gpsimd.tensor_tensor(WL[:, h % 2, :, :], raw_pair((1, 0)[f % 2], h // 2)[:, 8 * (h % 2):8 * (h % 2) + 8, :], WH[:, h % 2, :, :].bitcast(F32), ALU.subtract).then_inc(s["w_lo"], 1)

        def upper8(act, c, raw, half):
            act.wait_ge(s["w_used"], c - 1)
            nc.scalar.copy(WH[:, half, :, :], raw).then_inc(s["w_hi"], 1)

        def lower8(pool, c, raw, half):
            pool.wait_ge(s["w_hi"], c + 1)
            nc.gpsimd.tensor_tensor(WL[:, half, :, :], raw, WH[:, half, :, :].bitcast(F32), ALU.subtract).then_inc(s["w_lo"], 1)

        def raw_unit(slot):
            return WRAW[:, slot, :].rearrange("p (k c) -> p k c", c=P)

        def raw_pair(pslot, j):
            return WRAW[:, 2 * pslot:2 * pslot + 2, :].rearrange("p s (k c) -> p (s k c)", c=P).rearrange("p (k c) -> p k c", c=256)[:, :, j * P:(j + 1) * P]

        @block.gpsimd
        def _(pool):
            for h in range(2):
                lower(pool, h, raw_unit(0)[:, :, 0:112], h, 112)
            pool.wait_ge(free[0], 10)
            pool.wait_ge(free[1], 10)
            for k in range(1, KT):
                if k == 1:
                    pool.wait_ge(s["sq_D"], 1)
                    pool.wait_ge(s["sq_A"], 1)
                    nc.gpsimd.tensor_tensor(sqsum[:, :], sq[:, 0, :], sq[:, 1, :], ALU.add).then_inc(s["ss_done"], 2)
                else:
                    pool.wait_ge(s["sq_A"] if k % 2 else s["sq_D"], k // 2 + 1)
                    pool.wait_ge(s["ss_done"], k)
                    nc.gpsimd.tensor_tensor(sqsum[:, :], sqsum[:, :], sq[:, k % 3, :], ALU.add).then_inc(s["ss_done"], 1)
            with pool.Fori(0, 7) as q:
                for o in range(2):
                    for j in range(2):
                        for h in range(2):
                            lower(pool, 8 * q + 4 * o + 2 + 2 * j + h, raw_pair((o + 1) % 2, j), h)
            with pool.Fori(0, 8) as i:
                for n in range(6):
                    lower8(pool, 6 * i + 58 + n, raw3[:, n % 3, :, :], n % 2)
            with pool.Fori(0, 6) as i:
                for f in range(2):
                    for h in range(4):
                        lower_p(pool, 8 * i + (C3 + 4 * f + h), h, f, False)
            with pool.Fori(1, NG) as g:
                for f in range(6):
                    for h in range(4):
                        lower_p(pool, 24 * g + (C3 + 24 + 4 * f + h), h, f, f in (1, 2))
            for f in range(2):
                for h in range(4):
                    lower_p(pool, C3 + 24 * NG + 24 + 4 * f + h, h, f, True)

        def half_unit(pe, c, half, gslot, width=P, shift=0, ready=None):
            pe.wait_ge(s["w_lo"], c + 1)
            for k in range(8 * half, 8 * half + 8):
                if ready:
                    ready(k)
                for wt, act in ((WH, AH), (WH, AL), (WL, AH)):
                    for h in range(2):
                        last = nc.tensor.matmul(G[gslot][0:width, h, 0:HALF], wt[:, half, k % 8, 0:width], act[:, (k + shift) % KT, h * HALF:(h + 1) * HALF],
                                                start=(k == 0 and wt is WH and act is AH), stop=(k == KT - 1 and wt is WL))
            last.then_inc(s["w_used"], 1)

        @block.tensor
        def _(pe):
            mm, tr = nc.tensor.matmul, nc.tensor.transpose
            pe.wait_ge(s["c_in"], 32)
            for t in range(5):
                rows = P if t < 4 else NS
                pe.wait_ge(x_in[t], 16)
                for c in range(4):
                    name = ("x", 4 * t + c)
                    claim(pe, name)
                    for j in range(4):
                        last = tr(bank(name)[:, j * rows:(j + 1) * rows], xin[0:rows, t % 4, (4 * c + j) * P:(4 * c + j + 1) * P], ident[0:rows, 0:rows])
                    made(last, name)
            for h in range(2):
                half_unit(pe, h, h, 0, 112, ready=lambda k: pe.wait_ge(s["a_lo"], k + 1))
            pe.wait_ge(s["init"], 3)
            pe.wait_ge(s["ss_done"], KT)
            for h in range(2):
                made(mm(bank(f"ss{h}")[:, 0:HALF], ones[:, :], sqsum[:, h * HALF:(h + 1) * HALF], start=True, stop=True), f"ss{h}")
            def unit(u, prev_taken, side1=None, side2=None):
                pe.wait_ge(s["tile_taken"], u - 1)
                half_unit(pe, 2 * u, 0, u % 2)
                if side1:
                    side1()
                half_unit(pe, 2 * u + 1, 1, u % 2)
                if side2:
                    side2()

            def keys_by_token():
                pe.wait_ge(s["tile_taken"], 1)
                claim(pe, "kw0")
                for t in range(4):
                    last = tr(bank("kw0")[:, t * 112:(t + 1) * 112], kwd[:, t * P:(t + 1) * P], ident[0:112, 0:112])
                made(last, "kw0")
                claim(pe, "kw1")
                made(tr(bank("kw1")[0:NS, 0:112], kwd[:, NP:NT], ident[0:112, 0:112]), "kw1")

            def decay_by_token():
                pe.wait_ge(s["da_done"], 1)
                for j in range(3):
                    name = ("tok", j)
                    claim(pe, name)
                    for t in range(5):
                        rows = P if t < 4 else NS
                        last = tr(bank(name)[0:rows, t * NM:(t + 1) * NM], da[:, j, t * P:t * P + rows], ident[0:NM, 0:NM])
                    made(last, name)

            def keys_by_feature():
                pe.wait_ge(s["ki_n"], 1)
                claim(pe, "ki0")
                for t in range(4):
                    last = tr(bank("ki0")[:, t * P:(t + 1) * P], kin[:, t, :, :].rearrange("p e d -> p (e d)"), ident[:, :])
                made(last, "ki0")
                claim(pe, "ki1")
                made(tr(bank("ki1")[:, 0:NS], kin[0:NS, 4, :, :].rearrange("p e d -> p (e d)"), ident[0:NS, 0:NS]), "ki1")

            unit(1, 0)
            unit(2, 0)
            pe.wait_ge(s["c_in"], 16 * NCONST)
            claim(pe, "bd")
            made(mm(bank("bd")[0:NH, 0:REL], rbt[:, :], oh[:, :], start=True, stop=True), "bd")
            pe.wait_ge(s["stc_in"], 16)
            for g in range(3):
                claim(pe, ("sct", g))
                for m in range(4):
                    last = tr(bank(("sct", g))[:, m * 24:(m + 1) * 24], stc[:, (4 * g + m) * P:(4 * g + m + 1) * P], ident[0:24, 0:24])
                made(last, ("sct", g))
            keys_by_token()
            unit(3, 0)
            unit(4, 0, None, keys_by_feature)
            decay_by_token()
            for u in range(5, 9):
                unit(u, 0)

            def prompt_scores(hp):
                if hp == 0:
                    given(pe, "ki0")
                    given(pe, "ki1")
                pe.wait_ge(s["tile_taken"], hp + 2)
                for t in (1, 2, 3):
                    for e in range(2):
                        name = ("score", hp, t, e)
                        claim(pe, name)
                        made(mm(bank(name)[:, 0:(t + 1) * P], qi2[e * DI:(e + 1) * DI, hp, t * P:(t + 1) * P],
                                kit[e * DI:(e + 1) * DI, 0:(t + 1) * P], start=True, stop=True), name)

            def cached_scores(b):
                claim(pe, ("kcT", b))
                pe.wait_ge(kc_in[b % 4], 64 * (b // 4 + 1))
                for j in range(4):
                    last = tr(bank(("kcT", b))[0:DI, j * P:(j + 1) * P], kc[:, b % 4, j, :], ident[:, :])
                made(last, ("kcT", b))
                if b == 0:
                    pe.wait_ge(s["qis_done"], 2)
                given(pe, ("kcT", b))
                claim(pe, ("ss", b))
                made(mm(bank(("ss", b))[:, :], qis[:, b, :, :].rearrange("d h t -> d (h t)"), kcT[:, b % 2, :], start=True, stop=True), ("ss", b))

            def combine(b):
                if b == 0:
                    pe.wait_ge(s["wsel_done"], 1)
                    claim(pe, "comb")
                given(pe, ("ss", b))
                last = mm(bank("comb")[0:NS, :], wsel[:, b, :], rl[:, 2 + b % 2, :], start=(b == 0), stop=(b == NB - 1))
                if b == NB - 1:
                    made(last, "comb")
                else:
                    last.then_inc(s["rls_used"], 1)

            for z in range(8):
                def between(z=z):
                    prompt_scores(z)
                    if z:
                        combine(z - 1)
                unit(9 + z, 0, between, lambda z=z: cached_scores(z))
            combine(NB - 1)
            for g in range(2):
                claim(pe, f"new{g}")
                for h in range(8):
                    e = g
                    last = mm(bank(f"new{g}")[0:NS, h * NS:(h + 1) * NS], qi2[e * DI:(e + 1) * DI, h, NP:NT], kit[e * DI:(e + 1) * DI, NP:NT], start=True, stop=True)
                made(last, f"new{g}")
            with pe.Fori(0, 6) as i:
                for j in range(2):
                    u = 2 * i + 17 + j
                    pe.wait_ge(s["tile_taken"], u - 1)
                    half_unit(pe, 2 * u, 0, (17 + j) % 2)
                    half_unit(pe, 2 * u + 1, 1, (17 + j) % 2)
            def conv_tails():
                pe.wait_ge(s["cv_done"], 12)
                for g in range(3):
                    name = ("tail", g)
                    claim(pe, name)
                    for m in range(4):
                        last = tr(bank(name)[0:27, m * P:(m + 1) * P], tails[:, 4 * g + m, :], ident[:, :])
                    made(last, name)

            def product(i, n, mid=None):
                if n % 2 == 0:
                    pe.wait_ge(s["tile_taken"], 3 * i + (28 + n // 2))
                half_unit(pe, 6 * i + 58 + n, n % 2, (1, 0, 1)[n // 2], ready=(lambda k: mid() if k == 12 else None) if mid else None)

            def qk(i, t):
                tclaim(pe, f"qk{t}", i)
                tmade(mm(bank(f"qk{t}")[:, 0:(t + 1) * P], qT[:, t * P:(t + 1) * P], kT[:, 0:(t + 1) * P], start=True, stop=True), f"qk{t}")

            def by_token(i, name, src):
                for g in range(2):
                    tclaim(pe, f"{name}{g}", i)
                for g in range(2):
                    if g == 0:
                        for t in range(4):
                            last = tr(bank(f"{name}0")[:, t * P:(t + 1) * P], src[:, t * P:(t + 1) * P], ident[:, :])
                    else:
                        last = tr(bank(f"{name}1")[0:NS, 0:P], src[:, NP:NT], ident[:, :])
                    tmade(last, f"{name}{g}")

            def kca_t(i, b):
                a = i - 1
                tclaim(pe, f"kca{b}", i)
                pe.wait_ge(kca_in[b % 2], 256 * a + 64 * (b // 2 + 1))
                for j in range(4):
                    last = tr(bank(f"kca{b}")[:, j * P:(j + 1) * P], kca[:, b % 2, j, :], ident[:, :])
                tmade(last, f"kca{b}")

            def cached_logits(i, b):
                a = i - 1
                tgiven(pe, f"kca{b}", i)
                if b == 0:
                    tclaim(pe, "S", i)
                    pe.wait_ge(s["qpad_done"], a + 1)
                last = mm(bank("S")[0:NS, :], qpad[:, b, :], kcaT[:, b % 2, :], start=(b == 0), stop=(b == NB - 1))
                if b == NB - 1:
                    tmade(last, "S")
                else:
                    last.then_inc(s["kq"], 1)

            def state_t(i, g):
                tclaim(pe, f"hTb{g}", i)
                for b in range(4):
                    last = tr(bank(f"hTb{g}")[:, b * P:(b + 1) * P], h0[:, 4 * g + b, :], ident[:, :])
                tmade(last, f"hTb{g}")

            def y_chunk(i, c):
                tclaim(pe, f"y{c}", i)
                pe.wait_ge(s["mt_done"], 10 * i + 2 * c + 2)
                for e in range(2):
                    last = mm(bank(f"y{c}")[e * DS:(e + 1) * DS, 0:P], xtok[:, c, e * DS:(e + 1) * DS], mt[:, (2 * c + e) % 4, :], start=True, stop=True)
                if c:
                    pe.wait_ge(s["hT_done"], 4 * i + c)
                    last = mm(bank(f"y{c}")[:, P:2 * P], hT[:, c - 1, :], cf[:, c * P:(c + 1) * P], start=True, stop=True)
                tmade(last, f"y{c}")

            def y_decode(i):
                tclaim(pe, "ys", i)
                pe.wait_ge(s["mt_done"], 10 * i + 10)
                tgiven(pe, "hTb1", i)
                for b in range(NB):
                    mm(bank("ys")[:, P + b * NQ:P + (b + 1) * NQ], hTb[:, b, :], cf[:, NP + b * NQ:NP + (b + 1) * NQ], start=True, stop=True)
                for e in range(2):
                    last = mm(bank("ys")[e * DS:(e + 1) * DS, 0:NS], xtok[0:NS, 4, e * DS:(e + 1) * DS], mt[0:NS, e, 0:NS], start=True, stop=True)
                tmade(last, "ys")

            def turn_pe(i, att=True, units=True, mamba=True):
                a = i - 1
                early = isinstance(i, int) and i == 0
                if att:
                    pe.wait_ge(s["tile_taken"], 3 * i + 29)
                    qk(i, 0)
                    qk(i, 1)
                if units:
                    product(i, 0)
                    if early:
                        for n in range(1, 4):
                            if n == 1:
                                conv_tails()
                            product(i, n)
                        pe.wait_ge(s["h_init"], 4)
                if att:
                    qk(i, 2)
                    qk(i, 3)
                    tclaim(pe, "lnew", i)
                    tmade(mm(bank("lnew")[0:NS, 0:NS], qT[:, NP:NT], kT[:, NP:NT], start=True, stop=True), "lnew")
                if mamba:
                    pe.wait_ge(s["ssm_in"], LOADS * (i + 1))
                    by_token(i, "xtok", xs)
                if units and not early:
                    product(i, 1)
                if mamba:
                    by_token(i, "btok", bf)
                if att:
                    by_token(i, "ktok", kT)
                if mamba:
                    tclaim(pe, "cb0", i)
                    for c in range(4):
                        last = mm(bank("cb0")[:, c * P:(c + 1) * P], bf[:, c * P:(c + 1) * P], cf[:, c * P:(c + 1) * P], start=True, stop=True)
                    tmade(last, "cb0")
                    tclaim(pe, "cb1", i)
                    tmade(mm(bank("cb1")[0:NS, 0:NS], bf[:, NP:NT], cf[:, NP:NT], start=True, stop=True), "cb1")
                if att:
                    kca_t(i, 0)
                    kca_t(i, 1)
                if mamba:
                    tclaim(pe, "su", i)
                    pe.wait_ge(s["xw_done"], i + 1)
                    tgiven(pe, "btok1", i)
                    tgiven(pe, "btok0", i)
                    for c in range(4):
                        last = mm(bank("su")[:, c * P:(c + 1) * P], btok[:, c, :], xw[:, c, :], start=True, stop=True)
                    tmade(last, "su")
                if units and not early:
                    product(i, 2)
                if att:
                    cached_logits(i, 0)
                    cached_logits(i, 1)
                    kca_t(i, 2)
                if mamba:
                    state_t(i, 0)
                if att:
                    kca_t(i, 3)
                if mamba:
                    y_chunk(i, 0)
                if units and not early:
                    product(i, 3)
                if att:
                    cached_logits(i, 2)
                    cached_logits(i, 3)
                    kca_t(i, 4)
                if mamba:
                    state_t(i, 1)
                if att:
                    kca_t(i, 5)
                if mamba:
                    y_chunk(i, 1)
                if att:
                    by_token(i, "vtok", vT)
                if mamba:
                    y_chunk(i, 2)
                if units:
                    product(i, 4)
                if att:
                    cached_logits(i, 4)
                    cached_logits(i, 5)
                    kca_t(i, 6)
                if mamba:
                    y_chunk(i, 3)
                if att:
                    kca_t(i, 7)
                    probs_t(i, 0)
                if mamba:
                    y_decode(i)
                if att:
                    cached_logits(i, 6)
                    cached_logits(i, 7)

                def rest():
                    if att:
                        probs_t(i, 1)
                        values(i, 0)
                    if mamba:
                        update(i, 0)
                    if att:
                        probs_t(i, 2)
                        values(i, 1)
                    if mamba:
                        update(i, 1)
                    if att:
                        probs_t(i, 3)
                        values(i, 2)
                    if mamba:
                        tclaim(pe, "fin", i)
                        pe.wait_ge(s["hT_done"], 4 * i + 4)
                        tmade(tr(bank("fin")[:, 0:P], hT[:, 3, :], ident[:, :]), "fin")
                    if att:
                        values(i, 3)
                if units:
                    product(i, 5, rest)
                else:
                    rest()
                if att:
                    tclaim(pe, "pts", i)
                    tclaim(pe, "pvs", i)
                    pe.wait_ge(s["prob"], 5 * a + 5)
                    mm(bank("pts")[:, 5 * NS:6 * NS], ident[:, :], ident[:, 0:NS], start=True, stop=True)
                    for j in range(4):
                        tr(bank("pts")[:, j * NS:(j + 1) * NS], lgs[:, j * P:(j + 1) * P], ident[0:NS, 0:NS])
                    tmade(tr(bank("pts")[0:NS, 4 * NS:5 * NS], lgs[:, NP:NT], ident[0:NS, 0:NS]), "pts")
                    tgiven(pe, "pts", i)
                    pe.wait_ge(s["vca_in"], 512 * a + 512)
                    out = bank("pvs")
                    mm(out[:, 0:NS], vtok[0:NS, 4, :], pts[0:NS, 4, :], start=True, stop=False)
                    for b in range(NB):
                        for j in range(4):
                            last = mm(out[:, b * NQ:(b + 1) * NQ], vca[:, b, j, :], pts[:, j, b * NQ:(b + 1) * NQ], start=False, stop=(b == NB - 1 and j == 3))
                    tmade(last, "pvs")

            def update(i, g):
                tclaim(pe, f"us{g}", i)
                pe.wait_ge(s["bblk"], i + 1)
                tmade(mm(bank(f"us{g}")[:, :], xw[0:NS, 4, :], hTb[0:NS, 4 * g:4 * g + 4, :].rearrange("p b n -> p (b n)"), start=True, stop=True), f"us{g}")

            def probs_t(i, t):
                tclaim(pe, f"pt{t}", i)
                pe.wait_ge(s["prob"], 5 * (i - 1) + t + 1)
                for j in range(t + 1):
                    last = tr(bank(f"pt{t}")[:, j * P:(j + 1) * P], lg[:, PT_OFF[t] + j * P:PT_OFF[t] + (j + 1) * P], ident[:, :])
                tmade(last, f"pt{t}")

            def values(i, t):
                tclaim(pe, f"pv{t}", i)
                tgiven(pe, f"pt{t}", i)
                for j in range(t + 1):
                    last = mm(bank(f"pv{t}")[:, 0:P], vtok[:, j, :], pt[:, t % 2, j * P:(j + 1) * P], start=(j == 0), stop=(j == t))
                tmade(last, f"pv{t}")

            turn_pe(0, att=False)
            with pe.Fori(1, 8) as i:
                turn_pe(i)
            pe.wait_ge(s["link_s"], 4 * 8)
            pe.wait_ge(s["h_init"], 5)
            for h in range(2):
                claim(pe, f"ssy{h}")
                made(mm(bank(f"ssy{h}")[:, 0:HALF], ones[:, :], ssq[:, h * HALF:(h + 1) * HALF], start=True, stop=True), f"ssy{h}")
            turn_pe(8, units=False, mamba=False)

            def norm_sum():
                pe.wait_ge(s["ssf_used"], KT)
                for h in range(2):
                    claim(pe, f"ssf{h}")
                    made(mm(bank(f"ssf{h}")[:, 0:HALF], ones[:, :], acc[:, h * HALF:(h + 1) * HALF], start=True, stop=True), f"ssf{h}")
            for n in range(KT):
                pe.wait_ge(s["tile_taken"], T3 + n - 1)
                for h in range(2):
                    ready = (lambda k: pe.wait_ge(s["mix_lo"], k + 1)) if n == 0 else None
                    half_unit(pe, C3 + 2 * n + h, h, (T3 + n) % 2, shift=8, ready=ready)

            def unit_f(c, T, slot, ready=None):
                pe.wait_ge(s["tile_taken"], T - 1)
                for h in range(2):
                    half_unit(pe, c + h, h, slot, ready=ready)

            def down_half(c, half, T, slot):
                pe.wait_ge(s["w_lo"], c + 1)
                for t in range(2):
                    pe.wait_ge(s["tile_taken"], T + t - 1)
                    for k in range(4):
                        for wt, act in ((WH, hh), (WH, hl), (WL, hh)):
                            for h in range(2):
                                last = mm(G[(slot + t) % 2][:, h, 0:HALF], wt[:, half, 2 * k + t, :], act[:, k, h * HALF:(h + 1) * HALF],
                                          start=(k == 0 and wt is WH and act is hh), stop=(k == 3 and wt is WL))
                    last.then_inc(s["w_used"] if t else s["d_tile"], 1)
            for u in range(8):
                def follow(k):
                    pe.wait_ge(s["f_lo"], k + 1)
                    if k == 8:
                        norm_sum()
                unit_f(C3 + 32 + 2 * u, TF + u, (TF + u) % 2, follow if u == 0 else None)
            T1 = TF + 8
            with pe.Fori(1, NG) as g:
                c, T, slot, half = 24 * g + (C3 + 24), 24 * g + (T1 - 24), T1, 0
                for f in range(6):
                    if f in (1, 2):
                        if f == 1:
                            pe.wait_ge(s["hl_done"], 4 * g)
                        for h in range(4):
                            down_half(c + h, h % 2, T, slot)
                            T, slot = T + 2, slot + 2
                    else:
                        for u in range(2):
                            unit_f(c + 2 * u, T, slot % 2)
                            T, slot = T + 1, slot + 1
                    c = c + 4

            def last_sum():
                pe.wait_ge(s["fss_used"], KT)
                claim(pe, "fss")
                pe.wait_ge(s["pick_done"], 1)
                for t in (0, 4, 3, 2, 1):
                    rows = P if t < 4 else NS
                    last = mm(bank("fss")[0:rows, 0:5], acc[:, t * P:t * P + rows], pick[:, 4 - t:9 - t], start=(t == 0), stop=(t == 1))
                made(last, "fss")

            def back(m):
                pe.wait_ge(s["o_scaled"], 4 * m + 4)
                for t in range(5):
                    name = ("y", m, t)
                    rows = P if t < 4 else NS
                    claim(pe, name)
                    for j in range(4):
                        last = tr(bank(name)[0:rows, j * P:(j + 1) * P], XR[:, 4 * m + j, t * P:t * P + rows], ident[:, :])
                    made(last, name)
            pe.wait_ge(s["hl_done"], 4 * NG)
            for h in range(8):
                T = T1 + 24 * (NG - 1) + 2 * h
                down_half(C3 + 24 * NG + 24 + h, h % 2, T, T)
                if h in (3, 5, 7):
                    back((h - 3) // 2)
            last_sum()
            back(3)

        @block.scalar
        def _(act):
            copy, actv = nc.scalar.copy, nc.scalar.activation
            for n in range(0, 20, 2):
                t, c = n // 4, n % 4
                rows = P if t < 4 else NS
                wait(act, ("x", n))
                ins = copy(XR[:, 4 * c:4 * c + 4, t * P:t * P + rows], bank(("x", n))[:, 0:4 * rows].rearrange("p (a b) -> p a b", a=4))
                taken(ins, ("x", n))
            act.wait_ge(free[0], 10)
            act.wait_ge(free[1], 10)
            act.wait_ge(s["c_in"], 32)
            act.wait_ge(w_in[0], 32)
            for h in range(2):
                upper(act, h, raw_unit(0)[:, :, 0:112], h, 112)
            for k in range(KT):
                actv(AH[:, k, :], XR[:, k, :], ACT.Copy, scale=g_attn[:, k:k + 1]).then_inc(s["a_hi"], 1)
                if k % 2:
                    if k >= 3:
                        act.wait_ge(s["ss_done"], k - 2)
                    actv(sq[:, k % 3, :], XR[:, k, :], ACT.Square).then_inc(s["sq_A"], 1)

            def hi(c):
                p, j, h = (c + 2) // 4, (c - 2) % 4 // 2, c % 2
                if (c - 2) % 4 == 0:
                    act.wait_ge(w_in[p % 2], 16 * (p // 2 + 2) if p % 2 == 0 else 16 * (p // 2 + 1))
                upper(act, c, raw_pair(p % 2, j), h)
            hi(2)
            act.wait_ge(s["init"], 3)
            for h in range(2):
                wait(act, f"ss{h}")
                ins = actv(rstd[:, h, :], bank(f"ss{h}")[:, 0:HALF], ACT.Sqrt, bias=eps[:, :], scale=1.0 / DM)
                taken(ins, f"ss{h}")
            for c in range(3, 8):
                hi(c)
            act.wait_ge(s["c_in"], 16 * NCONST)
            actv(dvec[:, 2:3], dvec[:, 1:2], ACT.Exp).then_inc(s["dt_a"], 1)
            wait(act, "bd")
            ins = copy(bdt[:, :], bank("bd")[0:NH, 0:REL])
            taken(ins, "bd")
            for g in range(3):
                wait(act, ("sct", g))
                ins = copy(sct[:, 4 * g:4 * g + 4, :], bank(("sct", g))[:, 0:96].rearrange("p (a b) -> p a b", a=4))
                taken(ins, ("sct", g))
            act.wait_ge(s["init"], 4)
            for g in range(2):
                wait(act, f"kw{g}")
                ins = (copy(kwt[:, 0:4, :], bank("kw0")[:, 0:448].rearrange("p (a b) -> p a b", a=4)) if g == 0
                       else copy(kwt[0:NS, 4, :], bank("kw1")[0:NS, 0:112]))
                taken(ins, f"kw{g}")
            hi(8)
            act.wait_ge(s["dt_b"], 1)
            actv(dtmp[:, 2, :], dtmp[:, 1, :], ACT.Exp).then_inc(s["dt_a"], 1)
            act.wait_ge(s["dt_b"], 2)
            actv(dtmp[:, 3, :], dtmp[:, 3, :], ACT.Ln).then_inc(s["dt_a"], 1)
            hi(9)
            act.wait_ge(s["dt_b"], 3)
            actv(da[:, 2, :], da[:, 2, :], ACT.Exp).then_inc(s["dt_a"], 1)
            act.wait_ge(s["ki_ms"], 1)
            actv(small[:, 8:13], small[:, 0:5], ACT.Sqrt, bias=eps[:, :], scale=1.0 / DI).then_inc(s["ki_rt"], 1)
            hi(10)
            hi(11)
            for g in range(2):
                wait(act, f"ki{g}")
                ins = copy(kit[:, g * NP:NP + g * NS], bank(f"ki{g}")[:, 0:NS if g else NP])
                taken(ins, f"ki{g}")
            for j in range(3):
                wait(act, ("tok", j))
                copy(tokd[:, 0:4, j, :], bank(("tok", j))[:, 0:64].rearrange("p (a b) -> p a b", a=4))
                ins = copy(tokd[0:NS, 4, j, :], bank(("tok", j))[0:NS, 64:80])
                taken(ins, ("tok", j))

            for c in range(12, 19):
                hi(c)
            n = 0
            act.wait_ge(s["da_st"], 1)
            for z in range(8):
                hi(19 + 2 * z)
                for t in (1, 2, 3):
                    for e in range(2):
                        name = ("score", z, t, e)
                        wait(act, name)
                        if n >= 2:
                            act.wait_ge(s["rl_used"], n - 1)
                        ins = actv(rl[:, n % 2, 0:(t + 1) * P], bank(name)[:, 0:(t + 1) * P], ACT.Relu)
                        taken(ins, name)
                        n += 1
                hi(20 + 2 * z)
                wait(act, ("kcT", z))
                if z >= 2:
                    wait(act, ("ss", z - 2))
                ins = copy(kcT[:, z % 2, :], bank(("kcT", z))[0:DI, :])
                taken(ins, ("kcT", z))
                wait(act, ("ss", z))
                if z >= 2:
                    act.wait_ge(s["rls_used"], z - 1)
                ins = actv(rl[:, 2 + z % 2, :], bank(("ss", z))[:, :], ACT.Relu)
                taken(ins, ("ss", z))
                act.wait_ge(s["tile_taken"], z + 10)
                actv(ev[:, z % 2, :, :], ev[:, z % 2, :, :], ACT.Silu).then_inc(s["ev_silu"], 1)
                act.wait_ge(s["ev_silu"], z + 1)
                act.dma_start(zS[z], ev[:, z % 2, :, :].rearrange("p a b -> p (a b)")).then_inc(ev_st[z % 2], 16)
            for g in range(2):
                wait(act, f"new{g}")
                act.wait_ge(s["rl_used"], n + g - 1)
                ins = actv(rl[0:NS, g, :], bank(f"new{g}")[0:NS, :], ACT.Relu)
                taken(ins, f"new{g}")
            def hi3(i, n):
                act.wait_ge(r_in[n % 3], 32 * i + 16 * (n // 3) + 16)
                upper8(act, 6 * i + 58 + n, raw3[:, n % 3, :, :], n % 2)
            for m in range(-1, 12):
                if m < 11:
                    hi(37 + 2 * m)
                if m < 10:
                    hi(38 + 2 * m)
                else:
                    hi3(0, m - 10)
                if m < 0:
                    continue
                act.wait_ge(s["cv_done"], m + 1)
                actv(ev[:, m % 2, :, :], ev[:, m % 2, :, :], ACT.Silu).then_inc(s["cv_silu"], 1)
                act.wait_ge(s["cv_silu"], m + 1)
                act.dma_start(xcS[m], ev[:, m % 2, :, :].rearrange("p a b -> p (a b)")).then_inc(ev_st[m % 2], 16)
            for n in range(2, 4):
                hi3(0, n)
            for g in range(3):
                wait(act, ("tail", g))
                ins = copy(tailT[:, g * 512:(g + 1) * 512], bank(("tail", g))[0:27, :])
                taken(ins, ("tail", g))
            for g in range(2):
                given(act, ("tail", g))
            act.wait_ge(ev_st[0], 160)
            act.wait_ge(ev_st[1], 160)
            act.wait_ge(s["tail_out"], 32)
            act.wait_ge(s["h_init"], 4)

            def evac(i, name, dst, src):
                twait(act, name, i)
                ttaken(copy(dst, src), name)

            def evac_tokens(i, name, dst):
                evac(i, f"{name}0", dst[:, 0:4, :], bank(f"{name}0")[:, :].rearrange("p (t c) -> p t c", t=4))
                evac(i, f"{name}1", dst[0:NS, 4, :], bank(f"{name}1")[0:NS, 0:P])

            def exp_logits(i, t):
                a = i - 1
                act.wait_ge(s["nmax"], 5 * a + t + 1)
                v = lgs[:, :] if t == 4 else lg[:, PT_OFF[t]:PT_OFF[t] + (t + 1) * P]
                rows = NS if t == 4 else P
                actv(v, v, ACT.Exp, bias=stat[0:rows, 0, t:t + 1], accum_out=stat[0:rows, 1, t:t + 1]).then_inc(s["expd"], 1)

            def exp_decay(i, n):
                act.wait_ge(s["seg"], 10 * i + n + 1)
                rows = P if n < 8 else NS
                actv(ex[0:rows, n % 2, 0:rows], ex[0:rows, n % 2, 0:rows], ACT.Exp).then_inc(s["exd"], 1)

            def store_tokens(a, name, src, done, evd, n):
                for g in range(2):
                    tgiven(act, f"{name}{g}", a + 1)
                act.dma_start(O[f"{n}_prompt"].rearrange("(t p) c -> p t c", p=P)[:, :, bass.ds(a * DH, DH)], src[:, 0:4, :]).then_inc(done, 16)
                act.dma_start(O[f"{n}_sample"][:, bass.ds(a * DH, DH)], src[0:NS, 4, :]).then_inc(done, 16)

            def evac_cached(i, b):
                if b >= 2:
                    act.wait_ge(s["kq"], 7 * (i - 1) + b - 1)
                evac(i, f"kca{b}", kcaT[:, b % 2, :], bank(f"kca{b}")[:, :])

            def turn_act(i, att=True, units=True, mamba=True, nxt=True):
                a = i - 1
                later = not (isinstance(i, int) and i == 0)
                latera = not (isinstance(i, int) and i <= 1)
                early = not later
                if units and not early:
                    hi3(i, 1)
                if att:
                    exp_logits(i, 0)
                    exp_logits(i, 1)
                if units and not early:
                    hi3(i, 2)
                if mamba:
                    act.wait_ge(s["ssm_in"], LOADS * (i + 1))
                    actv(ea[:, :], ea[:, :], ACT.Exp).then_inc(s["ea_done"], 1)
                    for e in range(2):
                        ins = actv(elt[:, e, :].rearrange("p (c j) -> p c j", j=1), abc[:, e, 0:NP].rearrange("p (c j) -> p c j", j=P)[:, :, P - 1:P], ACT.Exp)
                        ins.then_inc(s["ea_done"], 1)
                    if later:
                        act.wait_ge(s["xw_done"], i)
                    evac_tokens(i, "xtok", xtok)
                if att:
                    exp_logits(i, 2)
                    exp_logits(i, 3)
                if units and not early:
                    hi3(i, 3)
                if mamba:
                    if later:
                        act.wait_ge(s["bblk"], i)
                    evac_tokens(i, "btok", btok)
                if att:
                    if latera:
                        act.wait_ge(s["kout"], 32 * a)
                    evac_tokens(i, "ktok", ktok)
                    evac_cached(i, 0)
                    evac_cached(i, 1)
                if mamba:
                    for n in range(4):
                        exp_decay(i, n)
                if att:
                    store_tokens(a, "ktok", ktok, s["kout"], None, "k")
                if units:
                    hi3(i, 4)
                if att:
                    evac_cached(i, 2)
                if mamba:
                    evac(i, "hTb0", hTb[:, 0:4, :].rearrange("p b n -> p (b n)"), bank("hTb0")[:, :])
                if att:
                    evac_cached(i, 3)
                if mamba:
                    exp_decay(i, 4)
                    exp_decay(i, 5)
                if units:
                    hi3(i, 5)
                if att:
                    evac_cached(i, 4)
                if mamba:
                    evac(i, "hTb1", hTb[:, 4:8, :].rearrange("p b n -> p (b n)"), bank("hTb1")[:, :])
                if att:
                    evac_cached(i, 5)
                if mamba:
                    exp_decay(i, 6)
                    exp_decay(i, 7)
                if att:
                    if latera:
                        act.wait_ge(s["vout"], 32 * a)
                        act.wait_ge(s["mixa"], 16 * a)
                    evac_tokens(i, "vtok", vtok)
                if mamba:
                    exp_decay(i, 8)
                    exp_decay(i, 9)
                if units and nxt:
                    hi3(i + 1, 0)
                if att:
                    evac_cached(i, 6)
                    evac_cached(i, 7)
                    store_tokens(a, "vtok", vtok, s["vout"], None, "v")
                    for t in range(4):
                        if t >= 2:
                            twait(act, f"pv{t - 2}", i)
                        evac(i, f"pt{t}", pt[:, t % 2, 0:(t + 1) * P], bank(f"pt{t}")[:, 0:(t + 1) * P])
                        evac(i, f"pv{t}", attT[:, t * P:(t + 1) * P], bank(f"pv{t}")[:, 0:P])
                        if t == 2 and mamba:
                            if later:
                                act.wait_ge(s["finout"], 16 * i)
                            evac(i, "fin", fin, bank("fin")[:, 0:P])
                if mamba:
                    if not att:
                        if later:
                            act.wait_ge(s["finout"], 16 * i)
                        evac(i, "fin", fin, bank("fin")[:, 0:P])
                    tgiven(act, "fin", i)
                    act.dma_start(bass.AP(O["ssm_prompt"].tensor, i * (P * P), [[P, P], [1, P]]), fin).then_inc(s["finout"], 16)
                    act.wait_ge(s["y_done"], i + 1)
                    act.dma_start(bass.AP(mixS.tensor, i * (P * NT) + 8 * P * NT, [[NT, P], [1, NT]]), xs[:, :]).then_inc(s["ymix"], 16)
                if att:
                    exp_logits(i, 4)
                if mamba:
                    act.wait_ge(s["h_done"], 2 * i + 2)
                    act.dma_start(bass.AP(O["ssm_sample"].tensor, i * (P * P), [[P, P], [NM * DS * P, NB], [1, P]]), h0[:, :, :]).then_inc(s["hout"], 16)
                if att:
                    twait(act, "pts", i)
                    copy(pts[:, 0:4, :], bank("pts")[:, 0:4 * NS].rearrange("p (j q) -> p j q", j=4))
                    ttaken(copy(pts[0:NS, 4, :], bank("pts")[0:NS, 4 * NS:5 * NS]), "pts")
                    evac(i, "pvs", attT[:, NP:NT], bank("pvs")[:, 0:NS])
                    tgiven(act, "pvs", i)
                    act.dma_start(bass.AP(mixS.tensor, a * (P * NT), [[NT, P], [1, NT]]), attT[:, :]).then_inc(s["mixa"], 16)
            turn_act(0, att=False)
            turn_act(1)
            with act.Fori(2, 7) as i:
                turn_act(i)
            turn_act(7, nxt=False)
            for h in range(2):
                wait(act, f"ssy{h}")
                taken(actv(rstd[:, h, :], bank(f"ssy{h}")[:, 0:HALF], ACT.Sqrt, bias=eps[:, :], scale=1.0 / (NM * DS)), f"ssy{h}")
            turn_act(8, units=False, mamba=False)

            def hi_p(c, h, f, down=False):
                if h == 0:
                    act.wait_ge(w_ld[f % 2], 4 * (c - C3 - 4 * (f % 2)) + 32)
                upper_p(act, c, h, f, down)
            def odd_back(m):
                for t in (1, 3):
                    wait(act, ("y", m, t))
                    evac_y = copy(y_tok(t)[:, 512 * m:512 * m + 512], bank(("y", m, t))[:, :])
                    taken(evac_y, ("y", m, t))

            def last_squares(n):
                T = T3 + KT + 8 + 24 * (NG - 1) + n
                act.wait_ge(s["tile_taken"], T + 1)
                if n >= 2:
                    act.wait_ge(s["fss_used"], n - 1)
                actv(sqf[:, n % 2, :], XR[:, n, :], ACT.Square).then_inc(s["o_sq"], 1)
                act.wait_ge(s["o_sq"], n + 1)
                actv(XR[:, n, :], XR[:, n, :], ACT.Copy, scale=gains[:, 16 + n:17 + n]).then_inc(s["o_scaled"], 1)
            hi_p(C3, 0, 0)
            hi_p(C3 + 1, 1, 0)
            for j in range(KT):
                act.wait_ge(mx_in[j % 6], 16 * (j // 6 + 1))
                if j < 8:
                    act.wait_ge(s["y_norm"], j + 1)
                if j == 0:
                    act.wait_ge(s["w_used"], C3)
                copy(AH[:, (j + 8) % KT, :], mx[:, j % 6, :]).then_inc(s["m_hi"], 1)

            def squares(n):
                act.wait_ge(s["tile_taken"], T3 + n + 1)
                if n >= 2:
                    act.wait_ge(s["ssf_used"], n - 1)
                actv(sqf[:, n % 2, :], XR[:, n, :], ACT.Square).then_inc(s["sqf_done"], 1)
            for c in range(2, 34):
                hi_p(C3 + c, c % 4, c // 4)
                if c % 2 and c >= 3:
                    squares((c - 3) // 2)
            for k in range(KT):
                if k == 0:
                    act.wait_ge(s["tile_taken"], TF)
                actv(AH[:, k, :], XR[:, k, :], ACT.Copy, scale=gains[:, k:k + 1]).then_inc(s["f_hi"], 1)
            for h in range(2):
                wait(act, f"ssf{h}")
                taken(actv(rstd[:, h, :], bank(f"ssf{h}")[:, 0:HALF], ACT.Sqrt, bias=eps[:, :], scale=1.0 / DM), f"ssf{h}")

            def hidden(g, j, T, up):
                if up:
                    act.wait_ge(s["h_mul"], 4 * g + j + 1)
                    copy(hh[:, j, :], us[:, j % 2, :]).then_inc(s["hh_done"], 1)
                else:
                    act.wait_ge(s["tile_taken"], T + 1)
                    actv(gs[:, j % 2, :], gs[:, j % 2, :], ACT.Silu).then_inc(s["g_silu"], 1)
            for c in range(34, 50):
                f, h = (c - 32) // 4, c % 4
                if c < 48:
                    hi_p(C3 + c, h, f)
                if c % 2 and c < 49 or c == 49:
                    u = (c - 35) // 2
                    if u < 7:
                        hidden(0, 2 * (u // 4) + u % 2, TF + u, u // 2 % 2)
            with act.Fori(1, NG) as g:
                c0, T0 = 24 * g + (C3 + 24), 24 * g + (TF + 8 - 24)
                T = T0
                tail = lambda: hidden(g - 1, 3, None, True)
                for f in range(6):
                    down = f in (1, 2)
                    for h in range(4):
                        hi_p(c0 + (4 * f + h), h, f, down)
                        if h % 2 and tail:
                            tail()
                            tail = None
                        if not down and h == 3:
                            hidden(g, 2 * (f // 4), T, f in (3, 5)) if f in (0, 3) else hidden(g, 2, T, f == 5)
                        if not down and h == 3:
                            j = (0 if f in (0, 3) else 2) + 1
                            tail = (lambda j=j, T=T, up=f in (3, 5): hidden(g, j, T + 1, up))
                    T = T + (8 if down else 2)
            for c in range(8):
                hi_p(C3 + 24 * NG + 24 + c, c % 4, c // 4, True)
                if c == 1:
                    hidden(NG - 1, 3, None, True)
                if c >= 3:
                    for n in (2 * c - 6, 2 * c - 5):
                        last_squares(n)
                if c in (5, 7):
                    odd_back((c - 5) // 2)
            for n in range(10, KT):
                last_squares(n)
                if n == 13:
                    odd_back(2)
            wait(act, "fss")
            actv(rfin[:, 0:4], bank("fss")[:, 0:4], ACT.Sqrt, bias=eps[:, :], scale=1.0 / DM)
            taken(actv(rfin[0:NS, 4:5], bank("fss")[0:NS, 4:5], ACT.Sqrt, bias=eps[0:NS, :], scale=1.0 / DM), "fss")
            odd_back(3)

        @block.vector
        def _(dve):
            ts_, tt, stt, cp = nc.vector.tensor_scalar, nc.vector.tensor_tensor, nc.vector.scalar_tensor_tensor, nc.vector.tensor_copy
            chained = [0]

            def link(ins):
                chained[0] += 1
                ins.then_inc(s["chain"], 1)
                dve.wait_ge(s["chain"], chained[0])
            nc.vector.memset(ones[:, :], 1.0).then_inc(s["init"], 1)
            nc.vector.memset(eps[:, :], EPS).then_inc(s["init"], 1)
            nc.vector.memset(tokd[:, :, :, :], 0.0).then_inc(s["init"], 1)
            for n in range(1, 20, 2):
                t, c = n // 4, n % 4
                rows = P if t < 4 else NS
                wait(dve, ("x", n))
                taken(cp(XR[:, 4 * c:4 * c + 4, t * P:t * P + rows], bank(("x", n))[:, 0:4 * rows].rearrange("p (a b) -> p a b", a=4)), ("x", n))
            dve.wait_ge(free[0], 10)
            dve.wait_ge(free[1], 10)
            dve.wait_ge(s["c_in"], 32)
            for k in range(KT):
                if k % 2 == 0:
                    if k >= 3:
                        dve.wait_ge(s["ss_done"], k - 2)
                    tt(sq[:, k % 3, :], XR[:, k, :], XR[:, k, :], ALU.mult).then_inc(s["sq_D"], 1)
                dve.wait_ge(s["a_hi"], k + 1)
                stt(AL[:, k, :], XR[:, k, :], g_attn[:, k:k + 1], AH[:, k, :].bitcast(F32), ALU.mult, ALU.subtract).then_inc(s["a_lo"], 1)
            for h in range(2):
                given(dve, f"ss{h}")
            link(nc.vector.reciprocal(rstd[:, :, :], rstd[:, :, :]))
            dve.wait_ge(s["x_store"], 16)
            nc.vector.memset(kwt[:, :, :], 0.0).then_inc(s["init"], 1)
            dve.wait_ge(s["w_used"], 2)
            ins = tt(kwd[:, :].rearrange("p (a b) -> p a b", a=2), G[0][0:112, :, 0:HALF], rstd[0:112, :, :], ALU.mult)
            ins.then_inc(s["tile_taken"], 1)

            def take_qi(h):
                dve.wait_ge(s["w_used"], 2 * h + 4)
                ins = tt(qi2[:, h, :].rearrange("p (a b) -> p a b", a=2), G[(h + 1) % 2][:, :, 0:HALF], rstd[:, :, :], ALU.mult)
                ins.then_inc(s["tile_taken"], 1)
            take_qi(0)
            dve.wait_ge(s["dt_in"], 16)
            dve.wait_ge(s["c_in"], 16 * NCONST)
            dve.wait_ge(s["dt_a"], 1)
            link(ts_(dvec[:, 3:4], dvec[:, 2:3], -1.0, None, ALU.mult))
            link(ts_(dtmp[:, 0, :], dtmp[:, 0, :], dvec[:, 0:1], None, ALU.add))
            stt(dtmp[:, 1, :], dtmp[:, 0, :], -1.0, dtmp[:, 0, :], ALU.mult, ALU.min).then_inc(s["dt_b"], 1)
            take_qi(1)
            dve.wait_ge(s["dt_a"], 2)
            ts_(dtmp[:, 3, :], dtmp[:, 2, :], 1.0, None, ALU.add).then_inc(s["dt_b"], 1)
            dve.wait_ge(s["dt_b"], 2)
            link(ts_(da[:, 1, :], dtmp[:, 2, :], 1.0, None, ALU.add))
            link(nc.vector.reciprocal(da[:, 0, :], da[:, 1, :]))
            link(stt(da[:, 1, :], da[:, 1, :], 1.0, dtmp[:, 2, :], ALU.subtract, ALU.subtract))
            link(tt(da[:, 1, :], da[:, 1, :], da[:, 0, :], ALU.mult))
            dve.wait_ge(s["dt_a"], 3)
            link(tt(dtmp[:, 3, :], dtmp[:, 3, :], da[:, 1, :], ALU.subtract))
            link(stt(da[:, 0, :], dtmp[:, 0, :], 0.0, dtmp[:, 3, :], ALU.max, ALU.add))
            link(ts_(dtmp[:, 0, :], da[:, 0, :], dvec[:, 3:4], None, ALU.mult))
            link(nc.vector.memset(dtmp[:, 1, :], 1.0))
            link(nc.vector.memset(dtmp[:, 1, 0:NP].rearrange("p (c j) -> p c j", j=P)[:, :, 0:1], 0.0))
            link(nc.vector.memset(dtmp[:, 1, NP:NT].rearrange("p (c j) -> p c j", j=NQ)[:, :, 0:1], 0.0))
            link(nc.vector.tensor_tensor_scan(da[:, 1, :], dtmp[:, 1, :], dtmp[:, 0, :], 0.0, ALU.mult, ALU.add))
            for lo, hi, n in ((0, NP, P), (NP, NT, NQ)):
                v = da[:, 1, lo:hi].rearrange("p (c j) -> p c j", j=n)
                link(tt(da[:, 2, lo:hi].rearrange("p (c j) -> p c j", j=n), v[:, :, n - 1:n].to_broadcast([NM, (hi - lo) // n, n]), v, ALU.subtract))
            nc.vector.memset(small[:, 0:8], 0.0).then_inc(s["dt_b"], 1)
            dve.wait_ge(s["dt_a"], 4)
            tt(da[:, 2, :], da[:, 2, :], da[:, 0, :], ALU.mult).then_inc(s["da_done"], 1)
            given(dve, "kw0")
            given(dve, "kw1")
            dve.wait_ge(s["dt_b"], 3)
            link(tt(kin[:, :, 0, :], kwt[:, :, 0:DI], kwt[:, :, 0:DI], ALU.mult))
            nc.vector.reduce_sum(small[:, 0:5], kin[:, :, 0, :], AX.X).then_inc(s["ki_ms"], 1)
            link(cp(wtok[:, :, :], kwt[:, :, 64:80]))
            dve.wait_ge(s["ki_rt"], 1)
            link(nc.vector.reciprocal(small[:, 0:5], small[:, 8:13]))
            link(tt(kin[:, :, 1, :], kwt[:, :, 0:DI], small[:, 0:5].rearrange("p (a b) -> p a b", b=1).to_broadcast([P, 5, DI]), ALU.mult))
            link(tt(kin[:, :, 0, :], kin[:, :, 1, :], gk[:, :].rearrange("p (a b) -> p a b", a=1).to_broadcast([P, 5, DI]), ALU.mult))
            cp(kin[:, :, 1, :], kin[:, :, 0, :]).then_inc(s["ki_n"], 1)
            take_qi(2)
            dve.wait_ge(s["wcol_in"], 16 * NB)
            tt(wsel[:, :, :], selm[:, :, :], wcol[:, :].rearrange("p (a b) -> p a b", b=1).to_broadcast([P, NB, NS]), ALU.mult).then_inc(s["wsel_done"], 1)
            for h in range(3, 8):
                take_qi(h)
            dve.wait_ge(s["tile_taken"], 9)
            for e in range(2):
                if e:
                    dve.wait_ge(s["qis_in"], 16)
                src = (qtmp if e else qi2[0:DI, :, NP:NT])
                for b in range(NB):
                    ins = cp(qis[:, b, :, :].rearrange("d (h e) t -> d h e t", e=2)[:, :, e, :], src[:, :, b * NQ:(b + 1) * NQ])
                ins.then_inc(s["qis_done"], 1)
            dve.wait_ge(s["ac_out"], 16)
            given(dve, ("tok", 1))
            given(dve, ("tok", 2))
            nc.vector.memset(scs[:, :], 0.0).then_inc(s["da_st"], 1)
            n = 0
            OFF = {1: 0, 2: 256, 3: 640}
            used = 0
            for z in range(8):
                for t in (1, 2, 3):
                    for e in range(2):
                        w = (t + 1) * P
                        dst, src = sc[:, OFF[t]:OFF[t] + w], rl[:, n % 2, 0:w]
                        h = 2 * z + e
                        given(dve, ("score", z, t, e))
                        if h:
                            if n:
                                dve.wait_ge(s["rl_used"], n)
                            stt(dst, src, wtok[:, t, h:h + 1], dst, ALU.mult, ALU.add).then_inc(s["rl_used"], 1)
                        else:
                            ts_(dst, src, wtok[:, t, h:h + 1], None, ALU.mult).then_inc(s["rl_used"], 1)
                        n += 1
                dve.wait_ge(s["w_used"], 2 * z + 20)
                if z >= 2:
                    dve.wait_ge(ev_st[z % 2], 16 * (z // 2))
                ins = tt(ev[:, z % 2, :, :], G[(9 + z) % 2][:, :, 0:HALF], rstd[:, :, :], ALU.mult)
                ins.then_inc(s["tile_taken"], 1)
            dve.wait_ge(s["da_st"], 1)
            wait(dve, "comb")
            taken(cp(scs[:, 0:PAST], bank("comb")[0:NS, :]), "comb")
            for g in range(2):
                given(dve, f"new{g}")
                for h in range(8):
                    src = rl[0:NS, g, h * NS:(h + 1) * NS]
                    ins = stt(scs[:, PAST:NT], src, wtok[0:NS, 4, 2 * h + g:2 * h + g + 1], scs[:, PAST:NT], ALU.mult, ALU.add)
                    if h == 7:
                        ins.then_inc(s["rl_used"], 1)
                        dve.wait_ge(s["rl_used"], n + 1)
                    else:
                        link(ins)
                n += 1
            link(tt(scs[:, PAST:NT], scs[:, PAST:NT], smask[:, :], ALU.add))
            for t in (1, 2, 3):
                v = sc[:, OFF[t] + t * P:OFF[t] + (t + 1) * P]
                link(tt(v, v, dmask[:, :], ALU.add))

            def take_xbc(m):
                g = (17 + m) % 2
                dve.wait_ge(s["w_used"], 36 + 2 * m)
                j = m % 2
                tt(cb[:, j, 3:3 + HALF], G[g][:, 0, 0:HALF], rstd[:, 0, :], ALU.mult)
                tt(cb[:, j, 3 + HALF:3 + NP], G[g][:, 1, 0:NP - HALF], rstd[:, 1, 0:NP - HALF], ALU.mult)
                ins = tt(cs[:, j, :, 3:], G[g][:, 1, NP - HALF:HALF].rearrange("p (b t) -> p b t", b=NB), rstd[:, 1, NP - HALF:HALF].rearrange("p (b t) -> p b t", b=NB), ALU.mult)
                ins.then_inc(s["tile_taken"], 1)
                link(cp(cs[:, j, :, 0:3], sct[:, m, :].rearrange("p (b t) -> p b t", b=NB)))
                cp(tails[:, m, 0:3], cb[:, j, NP:NP + 3])
                cp(tails[:, m, 3:27].rearrange("p (b t) -> p b t", b=NB), cs[:, j, :, NQ:NQ + 3])
                if m >= 2:
                    dve.wait_ge(ev_st[j], 16 * (4 + m // 2))
                else:
                    dve.wait_ge(ev_st[j], 64)
                flat = ev[:, j, :, :].rearrange("p a b -> p (a b)")
                dp, ds_ = flat[:, 0:NP], flat[:, NP:NT].rearrange("p (b t) -> p b t", b=NB)
                ts_(dp, cb[:, j, 0:NP], convw[:, m, 0:1], convw[:, m, 4:5], ALU.mult, ALU.add)
                link(ts_(ds_, cs[:, j, :, 0:NQ], convw[:, m, 0:1], convw[:, m, 4:5], ALU.mult, ALU.add))
                for w in range(1, 4):
                    stt(dp, cb[:, j, w:w + NP], convw[:, m, w:w + 1], dp, ALU.mult, ALU.add)
                    ins = stt(ds_, cs[:, j, :, w:w + NQ], convw[:, m, w:w + 1], ds_, ALU.mult, ALU.add)
                    if w == 3:
                        ins.then_inc(s["cv_done"], 1)
                    else:
                        link(ins)

            m8 = small[:, 16:24]

            def pick_largest(r, part):
                if r < 3:
                    t, rows, w = r + 1, P, (r + 2) * P
                    src, k, dst = sc[:, OFF[t]:OFF[t] + w], TOPK_P, neg_p[:, PT_OFF[t]:PT_OFF[t] + w]
                else:
                    rows, w = NS, NT
                    src, k, dst = scs[:, :], TOPK_S, neg_s[:, :]
                rounds = -(-k // 8)
                lo, hi = part * rounds // 3, (part + 1) * rounds // 3
                for i in range(lo, hi):
                    link(nc.vector.max(m8[0:rows], src if i == 0 else work[0:rows, 0:w]))
                    if i < rounds - 1:
                        link(nc.vector.match_replace(work[0:rows, 0:w], m8[0:rows], src if i == 0 else work[0:rows, 0:w], MASKED))
                if part == 2:
                    thr = small[0:rows, 16 + (k - 1) % 8:17 + (k - 1) % 8]
                    cnt, need = small[0:rows, 32:33], small[0:rows, 33:34]
                    e_, g_, c_ = eqt[0:rows, 0:w], gtt[0:rows, 0:w], cum[0:rows, 0:w]
                    link(ts_(g_, src, thr, None, ALU.is_gt, ALU.add, accum_out=cnt))
                    link(ts_(need, cnt, -1.0, float(k), ALU.mult, ALU.add))
                    link(ts_(e_, src, thr, None, ALU.is_equal))
                    link(nc.vector.tensor_tensor_scan(c_, e_, e_, 0.0, ALU.add, ALU.max))
                    link(stt(c_, c_, need, e_, ALU.is_le, ALU.mult))
                    link(tt(g_, g_, c_, ALU.add))
                    ts_(dst, g_, 1.0, BIG, ALU.subtract, ALU.mult).then_inc(s["topk"], 1)
                    dve.wait_ge(s["topk"], r + 1)

            given(dve, ("sct", 2))
            link(nc.vector.memset(cb[:, :, 0:3], 0.0))
            parts = [(r, part) for r in range(4) for part in range(3)]
            for m in range(12):
                take_xbc(m)
                for _ in range((2, 1, 1, 1, 1, 1, 1, 1, 1, 1, 0, 0)[m]):
                    pick_largest(*parts.pop(0))
            for r, part in parts:
                pick_largest(r, part)

            dve.wait_ge(s["tail_out"], 32)
            for m in range(2):
                dve.wait_ge(ev_st[m], 160)
            for m in range(3):
                given(dve, ("tail", m))
            for v in (xtok, qpad, ssq, hTb):
                nc.vector.memset(v[:, :] if v is ssq else v[:, :, :], 0.0).then_inc(s["h_init"], 1)
            dve.wait_ge(s["h_init"], 4)
            dve.wait_ge(s["h_in"], 48)

            class Chain:

                def __init__(self, sem, per):
                    self.sem, self.per = sem, per

                def start(self, i):
                    self.i, self.n = i, 0

                def __call__(self, ins):
                    self.n += 1
                    ins.then_inc(self.sem, 1)
                    dve.wait_ge(self.sem, self.per * self.i + self.n)

                def end(self):
                    assert self.n == self.per, self.n
            la, ls = Chain(s["link_a"], 6), Chain(s["link_s"], 4)

            def take(i, n, dst):
                dve.wait_ge(s["w_used"], 6 * i + 60 + 2 * n)
                tt(dst[:, :].rearrange("p (a b) -> p a b", a=2), G[(1, 0, 1)[n]][:, :, 0:HALF], rstd[:, :, :], ALU.mult).then_inc(s["tile_taken"], 1)

            def logits(i, t):
                a = i - 1
                w = (t + 1) * P
                v = lg[:, PT_OFF[t]:PT_OFF[t] + w]
                twait(dve, f"qk{t}", i)
                ins = stt(v, bank(f"qk{t}")[:, 0:w], SCALE, neg_p[:, PT_OFF[t]:PT_OFF[t] + w], ALU.mult, ALU.add)
                ttaken(ins, f"qk{t}")
                tgiven(dve, f"qk{t}", i)
                near = min(w, 2 * P)
                tt(v[:, w - near:w], v[:, w - near:w], bias_p[:, 2 * P - near:2 * P], ALU.add).then_inc(s["lg_done"], 1)
                dve.wait_ge(s["lg_done"], 5 * a + t + 1)
                nc.vector.reduce_max(stat[:, 0, t:t + 1], v, AX.X, negate=True).then_inc(s["nmax"], 1)

            def normal(i, t):
                a = i - 1
                rows = NS if t == 4 else P
                v = lgs[:, :] if t == 4 else lg[:, PT_OFF[t]:PT_OFF[t] + (t + 1) * P]
                dve.wait_ge(s["expd"], 5 * a + t + 1)
                la(nc.vector.reciprocal(stat[0:rows, 2, t:t + 1], stat[0:rows, 1, t:t + 1]))
                ts_(v, v, stat[0:rows, 2, t:t + 1], None, ALU.mult).then_inc(s["prob"], 1)

            def seg(i, n):
                c, e = n // 2, n % 2
                rows = P if c < 4 else NS
                ts_(ex[0:rows, e, 0:rows], abc[0:rows, e, c * P:c * P + rows], colb[0:rows, c, 1, e:e + 1], 0.0, ALU.subtract, ALU.min).then_inc(s["seg"], 1)

            def weigh(i, n):
                c, e = n // 2, n % 2
                rows = P if c < 4 else NS
                dve.wait_ge(s["exd"], 10 * i + n + 1)
                if n >= 4 and e == 0:
                    twait(dve, f"y{c - 2}", i)
                stt(mt[0:rows, n % 4, 0:rows], ex[0:rows, e, 0:rows], colb[0:rows, c, 0, e:e + 1], cbm[0:rows, c, 0:rows], ALU.mult, ALU.mult).then_inc(s["mt_done"], 1)
                dve.wait_ge(s["mt_done"], 10 * i + n + 1)

            def take_y(i, c):
                name = f"y{c}" if c < 4 else "ys"
                lo, hi = (c * P, (c + 1) * P) if c < 4 else (NP, NT)
                twait(dve, name, i)
                if c:
                    tt(ea[:, lo:hi], ea[:, lo:hi], bank(name)[:, P:P + hi - lo], ALU.mult)
                ttaken(stt(xs[:, lo:hi], xs[:, lo:hi], dcol[:, :], bank(name)[:, 0:hi - lo], ALU.mult, ALU.add), name)

            def turn_dve(i, att=True, units=True, mamba=True):
                a = i - 1
                if att:
                    la.start(a)
                    dve.wait_ge(s["tile_taken"], 3 * i + 29)
                    cp(bass.AP(qpad, 0, [[NB * NS, P], [NS + NQ, NB], [1, NQ]]), qT[:, NP:NT].rearrange("p (b t) -> p b t", b=NB)).then_inc(s["qpad_done"], 1)
                    dve.wait_ge(s["bias_in"], 32 * a + 32)
                    logits(i, 0)
                    logits(i, 1)
                if att:
                    normal(i, 0)
                    normal(i, 1)
                    logits(i, 2)
                    logits(i, 3)
                    twait(dve, "lnew", i)
                    ttaken(stt(lgs[:, NP:NT], bank("lnew")[0:NS, 0:NS], SCALE, neg_s[:, NP:NT], ALU.mult, ALU.add), "lnew")
                    tgiven(dve, "lnew", i)
                    v = lgs[:, NP:NT].rearrange("p (b t) -> p b t", b=NB)
                    la(tt(v, v, bias_s[:, P:P + NQ].rearrange("p (b t) -> p b t", b=1).to_broadcast([NS, NB, NQ]), ALU.add))
                if mamba:
                    ls.start(i)
                    dve.wait_ge(s["ssm_in"], LOADS * (i + 1))
                    ls(cp(colb[:, :, :, :], tokd[:, :, :, bass.ds(2 * i, 2)]))
                    dve.wait_ge(s["ea_done"], 3 * i + 3)
                    cp(els[:, :].rearrange("p (b t) -> p b t", t=1), ea[:, NP:NT].rearrange("p (b t) -> p b t", t=NQ)[:, :, NQ - 1:NQ])
                    tgiven(dve, "xtok1", i)
                    tgiven(dve, "xtok0", i)
                    tt(xw[:, :, :].rearrange("p t (e d) -> p t e d", e=2), xtok[:, :, :].rearrange("p t (e d) -> p t e d", e=2),
                       colb[:, :, 2, :].rearrange("p t (e d) -> p t e d", d=1).to_broadcast([P, 5, 2, DS]), ALU.mult).then_inc(s["xw_done"], 1)
                    seg(i, 0)
                    seg(i, 1)
                if units:
                    take(i, 0, qT)
                if att:
                    normal(i, 2)
                    normal(i, 3)
                if mamba:
                    twait(dve, "cb0", i)
                    if not (isinstance(i, int) and i == 0):
                        dve.wait_ge(s["finout"], 16 * i)
                    ttaken(tt(cbm[:, 0:4, :], bank("cb0")[:, :].rearrange("p (c j) -> p c j", c=4), cmask[:, :].rearrange("p (c j) -> p c j", c=1).to_broadcast([P, 4, P]), ALU.mult), "cb0")
                    twait(dve, "cb1", i)
                    ttaken(tt(cbm[0:NS, 4, 0:NS], bank("cb1")[0:NS, 0:NS], bmask[:, :], ALU.mult), "cb1")
                    tgiven(dve, "cb1", i)
                    for n in range(4):
                        weigh(i, n)
                        seg(i, n + 2)
                    twait(dve, "su", i)
                    cp(hT[:, 0, :], bank("su")[:, 0:P]).then_inc(s["hT_done"], 1)
                    dve.wait_ge(s["hT_done"], 4 * i + 1)
                    for c in range(1, 4):
                        for e in range(2):
                            lo, hi = e * DS, (e + 1) * DS
                            ins = stt(hT[:, c, lo:hi], hT[:, c - 1, lo:hi], elt[:, e, c:c + 1], bank("su")[:, c * P + lo:c * P + hi], ALU.mult, ALU.add)
                        ins.then_inc(s["hT_done"], 1)
                        dve.wait_ge(s["hT_done"], 4 * i + 1 + c)
                    ttaken(cp(els[:, :], els[:, :]), "su")
                for c in range(4):
                    if mamba:
                        if c < 3:
                            for e in range(2):
                                weigh(i, 2 * c + 4 + e)
                                if 2 * c + 6 + e < 10:
                                    seg(i, 2 * c + 6 + e)
                        take_y(i, c)
                    if c == 0 and units:
                        take(i, 1, kT)
                if mamba:
                    take_y(i, 4)
                    tgiven(dve, "ys", i)
                    tgiven(dve, "btok1", i)
                    tt(hTb[0:NS, :, :], btok[0:NS, 4, :].rearrange("p (b n) -> p b n", b=1).to_broadcast([NS, NB, P]),
                       bmask8.to_broadcast([NS, NB, P]), ALU.mult).then_inc(s["bblk"], 1)
                if att:
                    twait(dve, "S", i)
                    ttaken(stt(lgs[:, 0:PAST], bank("S")[0:NS, :], SCALE, neg_s[:, 0:PAST], ALU.mult, ALU.add), "S")
                    tgiven(dve, "S", i)
                    tt(lgs[:, PAST - P:PAST], lgs[:, PAST - P:PAST], bias_s[:, 0:P], ALU.add).then_inc(s["lg_done"], 1)
                    dve.wait_ge(s["lg_done"], 5 * a + 5)
                    nc.vector.reduce_max(stat[0:NS, 0, 4:5], lgs[:, :], AX.X, negate=True).then_inc(s["nmax"], 1)
                if mamba:
                    ls(tt(xs[:, P:NT], xs[:, P:NT], ea[:, P:NT], ALU.add))
                    tt(xs[:, :], xs[:, :], sz[:, :], ALU.mult).then_inc(s["y_done"], 1)
                    for g in range(2):
                        twait(dve, f"us{g}", i)
                        for b in range(4):
                            ins = stt(h0[:, 4 * g + b, :], h0[:, 4 * g + b, :], els[:, 4 * g + b:4 * g + b + 1], bank(f"us{g}")[:, b * P:(b + 1) * P], ALU.mult, ALU.add)
                        ttaken(ins, f"us{g}")
                        tgiven(dve, f"us{g}", i)
                        cp(stat[:, 2, 6:7], els[:, 0:1]).then_inc(s["h_done"], 1)
                    dve.wait_ge(s["y_done"], i + 1)
                    ls(tt(ea[:, :], xs[:, :], xs[:, :], ALU.mult))
                    ls(tt(ssq[:, :], ssq[:, :], ea[:, :], ALU.add))
                    ls.end()
                if att:
                    normal(i, 4)
                    la.end()
                if units:
                    take(i, 2, vT)
            turn_dve(0, att=False)
            with dve.Fori(1, 8) as i:
                turn_dve(i)
            nc.vector.memset(ones[:, :], 1.0).then_inc(s["h_init"], 1)
            for h in range(2):
                given(dve, f"ssy{h}")
            dve.wait_ge(s["tile_taken"], T3)
            nc.vector.reciprocal(rstd[:, :, :], rstd[:, :, :]).then_inc(s["ry_done"], 1)
            turn_dve(8, units=False, mamba=False)

            dve.wait_ge(s["ry_done"], 1)

            def y_norm(j):
                v = mx[:, j % 6, :]
                dve.wait_ge(mx_in[j % 6], 16 * (j // 6 + 1))
                stt(v, v, gains[:, 32 + j:33 + j], rstd[:, :, :].rearrange("p a b -> p (a b)"), ALU.mult, ALU.mult).then_inc(s["y_norm"], 1)
            y_norm(0)
            y_norm(1)
            for j in range(KT):
                dve.wait_ge(s["m_hi"], j + 1)
                tt(AL[:, (j + 8) % KT, :], mx[:, j % 6, :], AH[:, (j + 8) % KT, :].bitcast(F32), ALU.subtract).then_inc(s["mix_lo"], 1)
                if j + 2 < 8:
                    y_norm(j + 2)
            two = lambda v: v.rearrange("p (a b) -> p a b", a=2)
            def add_squares(n, made_, used):
                dve.wait_ge(s[made_], n + 1)
                if n:
                    dve.wait_ge(s[used], n)
                    tt(acc, acc, sqf[:, n % 2, :], ALU.add).then_inc(s[used], 1)
                else:
                    cp(acc, sqf[:, 0, :]).then_inc(s[used], 1)

            for n in range(KT):
                dve.wait_ge(xt_in[n % 2], 16 * (n // 2 + 1))
                dve.wait_ge(s["w_used"], C3 + 2 * n + 2)
                tt(two(XR[:, n, :]), G[(T3 + n) % 2][:, :, 0:HALF], two(xt[:, n % 2, :]), ALU.add).then_inc(s["tile_taken"], 1)
                if n:
                    add_squares(n - 1, "sqf_done", "ssf_used")
            add_squares(KT - 1, "sqf_done", "ssf_used")
            dve.wait_ge(s["tile_taken"], TF)
            nc.vector.memset(pick[:, :], 0.0).then_inc(s["h_init"], 1)
            dve.wait_ge(s["h_init"], 6)
            nc.vector.memset(pick[:, 4:5], 1.0).then_inc(s["pick_done"], 1)

            for k in range(KT):
                dve.wait_ge(s["f_hi"], k + 1)
                stt(AL[:, k, :], XR[:, k, :], gains[:, k:k + 1], AH[:, k, :].bitcast(F32), ALU.mult, ALU.subtract).then_inc(s["f_lo"], 1)
            for h in range(2):
                given(dve, f"ssf{h}")
            nc.vector.reciprocal(rstd[:, :, :], rstd[:, :, :]).then_inc(s["ry_done"], 1)
            dve.wait_ge(s["ry_done"], 2)

            def take_f(g, j, c, T, slot, up, first=False):
                dst = (us if up else gs)[:, j % 2, :]
                if up and not (first and j < 2):
                    dve.wait_ge(s["hl_done"], 4 * g + j - 1)
                dve.wait_ge(s["w_used"], c + 2)
                tt(two(dst), G[slot % 2][:, :, 0:HALF], rstd[:, :, :], ALU.mult).then_inc(s["tile_taken"], 1)
                if up:
                    dve.wait_ge(s["tile_taken"], T + 1)
                    dve.wait_ge(s["g_silu"], 4 * g + j + 1)
                    tt(dst, dst, gs[:, j % 2, :], ALU.mult).then_inc(s["h_mul"], 1)
                    dve.wait_ge(s["hh_done"], 4 * g + j + 1)
                    tt(hl[:, j, :], dst, hh[:, j, :].bitcast(F32), ALU.subtract).then_inc(s["hl_done"], 1)

            def take_down(c, n, T, slot, tiles):
                if n % 2:
                    dve.wait_ge(s["w_used"], c + 1)
                else:
                    dve.wait_ge(s["d_tile"], tiles + n // 2 + 1)
                tt(two(XR[:, n, :]), G[slot % 2][:, :, 0:HALF], two(XR[:, n, :]), ALU.add).then_inc(s["tile_taken"], 1)
            def take_back(m, t):
                name = ("y", m, t)
                rows = P if t < 4 else NS
                wait(dve, name)
                taken(cp(y_tok(t)[:, 512 * m:512 * m + 512], bank(name)[0:rows, :]), name)
            for u in range(8):
                take_f(0, 2 * (u // 4) + u % 2, C3 + 32 + 2 * u, TF + u, TF + u, u // 2 % 2, True)
            T1 = TF + 8
            with dve.Fori(1, NG) as g:
                c, T, slot = 24 * g + (C3 + 24), 24 * g + (T1 - 24), T1
                for f in range(6):
                    if f in (1, 2):
                        for n in range(8 * f - 8, 8 * f):
                            take_down(c + (n % 8) // 2, n, T, slot, 8 * g - 8)
                            T, slot = T + 1, slot + 1
                    else:
                        for u in range(2):
                            take_f(g, (2 if f > 3 else 0) + u, c + 2 * u, T, slot, f in (3, 5))
                            T, slot = T + 1, slot + 1
                    c = c + 4
            for n in range(KT):
                T = T1 + 24 * (NG - 1) + n
                take_down(C3 + 24 * NG + 24 + n // 2, n, T, T, 8 * (NG - 1))
                if n > 1:
                    add_squares(n - 2, "o_sq", "fss_used")
                if n in (7, 11, 15):
                    for t in (0, 2, 4):
                        take_back(n // 4 - 1, t)
            for n in (14, 15):
                add_squares(n, "o_sq", "fss_used")
            given(dve, "fss")
            nc.vector.reciprocal(rfin[:, 0:4], rfin[:, 0:4]).then_inc(s["rfin_done"], 1)
            nc.vector.reciprocal(rfin[0:NS, 4:5], rfin[0:NS, 4:5]).then_inc(s["rfin_done"], 1)
            dve.wait_ge(s["rfin_done"], 2)
            for t in range(5):
                if t % 2 == 0:
                    take_back(3, t)
                rows = P if t < 4 else NS
                given(dve, ("y", 3, t))
                ts_(y_tok(t), y_tok(t), rfin[0:rows, t:t + 1], None, ALU.mult).then_inc(s["y_scaled"], 1)


def bucket(rel):
    rel = max(rel, 0)
    if rel < 16:
        return rel
    return min(16 + int(math.log(rel / 16) / math.log(8) * 16), 31)


def kernel(**inputs):
    import concourse.bacc as _bacc
    from concourse.bass_utils import run_bass_kernel_spmd as _run
    f = np.float32
    nc = _bacc.Bacc("TRN2", target_bir_lowering=False, num_devices=1)
    a = dict(inputs)
    arrays = {"x_prompt": a["x_prompt"][0], "x_sample": a["x_sample"].reshape(NS, DM), "w_in": a["w_in"][0],
              "norm_attn": a["norm_attn"][0], "idx_k_norm": a["idx_k_norm"][0],
              "cache_kidx": a["cache_kidx"][0].reshape(-1, DI), "state_conv": a["state_conv"][0].reshape(24, CONV),
              "page_table": a["page_table"].reshape(-1), "rel_bias": a["rel_bias"], "conv_w": a["conv_w"][0], "conv_b": a["conv_b"][0],
              "dt_bias": a["dt_bias"][0], "a_log": a["a_log"][0], "d_skip": a["d_skip"][0], "ssm_norm": a["ssm_norm"][0], "norm_ffn": a["norm_ffn"][0], "norm_final": a["norm_final"],
              "w_out": a["w_out"][0], "w_gate": a["w_gate"][0], "w_up": a["w_up"][0], "w_down": a["w_down"][0],
              "cache_k": a["cache_k"][0].reshape(-1, QKV), "cache_v": a["cache_v"][0].reshape(-1, QKV), "state_ssm": a["state_ssm"][0].reshape(-1, P)}
    onehot = np.zeros((32, REL), f)
    for j in range(REL):
        onehot[bucket(255 - j), j] += 1
        onehot[31, j] -= 1
    row = np.arange(P)
    tok = np.arange(NS)
    later = row[None, :] > row[:, None]
    sel = np.zeros((P, NB, NS), f)
    for b in range(NB):
        sel[row, b, b * NQ + row % NQ] = 1
    same = (tok[:, None] // NQ == tok[None, :] // NQ)
    arrays |= {"ident": np.eye(P, dtype=f), "onehot": onehot, "select_row": sel,
               "causal_score": np.where(later, f(MASKED), f(0)).astype(f), "causal_logit": np.where(later, f(-BIG), f(0)).astype(f),
               "causal_T": np.triu(np.ones((P, P), f)), "decode_T": (same & (tok[None, :] >= tok[:, None])).astype(f),
               "own_sequence": (tok[:, None] // NQ == np.arange(NB)[None, :]).astype(f),
               "decode_mask": np.where(same & (tok[None, :] <= tok[:, None]), f(0), f(MASKED)).astype(f)}
    arrays = {f"in_{k}": np.ascontiguousarray(v) for k, v in arrays.items()}
    I = {k[3:]: nc.dram_tensor(k, v.shape, mybir.dt.from_np(v.dtype), kind="ExternalInput").ap() for k, v in arrays.items()}
    outs = {"y_prompt": (NP, DM), "y_sample": (NS, DM), "kidx_prompt": (NP, DI), "kidx_sample": (NS, DI), "conv_prompt": (3, CONV), "conv_sample": (24, CONV),
            "k_prompt": (NP, QKV), "v_prompt": (NP, QKV), "k_sample": (NS, QKV), "v_sample": (NS, QKV),
            "ssm_prompt": (NM * DS, P), "ssm_sample": (NB * NM * DS, P)}
    O = {k: nc.dram_tensor(k, v, F32, kind="ExternalOutput").ap() for k, v in outs.items()}
    build(nc, I, O)
    r = _run(nc, [arrays], core_ids=[0]).results[0]
    shapes = (("y_prompt", (1, NP, DM)), ("y_sample", (NB, NQ, DM)), ("k_prompt", (1, 1, NP, NH, DH)), ("v_prompt", (1, 1, NP, NH, DH)),
              ("kidx_prompt", (1, 1, NP, DI)), ("conv_prompt", (1, 1, 3, CONV)), ("ssm_prompt", (1, 1, NM, DS, P)),
              ("k_sample", (1, NB, NQ, NH, DH)), ("v_sample", (1, NB, NQ, NH, DH)), ("kidx_sample", (1, NB, NQ, DI)),
              ("conv_sample", (1, NB, 3, CONV)), ("ssm_sample", (1, NB, NM, DS, P)))
    return tuple(r[n].reshape(v) for n, v in shapes)
```
